# Optimizing a Trainium2 kernel written in Bass

```python
import jax, jax.numpy as jnp
from jax import lax
import numpy as np
import math

D_MODEL = 1024
BATCH = 1
SEQ = 512
DEPTH = 1

MEM_LEN = 256
HEAD_DIM = 64
CONV_CH = D_MODEL // 4
ATTN_HEADS = (3 * D_MODEL // 4) // HEAD_DIM
ATTN_WIDTH = ATTN_HEADS * HEAD_DIM
MIX_WIDTH = CONV_CH + ATTN_WIDTH
IN_WIDTH = 2 * CONV_CH + 3 * ATTN_WIDTH
CONV_KERNEL = 31
DILATED_BRANCHES = ((128, 1), (512, 4), (2048, 16))
ROPE_THETA = 10000.0
MEM_HEADS = 4
MEM_HEAD_DIM = D_MODEL // MEM_HEADS
N_GROUPS = 4
EXPERTS_PER_GROUP = 8
N_EXPERTS = N_GROUPS * EXPERTS_PER_GROUP
TOP_K = 2
EXPERT_FF = D_MODEL // 2
DISPATCH_BLOCK = 256
NORM_EPS = 1e-6
LN_EPS = 1e-5


def rms_norm(t, g):
    tf = t.astype(jnp.float32)
    y = tf * lax.rsqrt(jnp.mean(tf * tf, axis=-1, keepdims=True) + NORM_EPS)
    return (y * g.astype(jnp.float32)).astype(t.dtype)

def layer_norm(t, g, b):
    tf = t.astype(jnp.float32)
    mu = jnp.mean(tf, axis=-1, keepdims=True)
    var = jnp.mean(jnp.square(tf - mu), axis=-1, keepdims=True)
    y = (tf - mu) * lax.rsqrt(var + LN_EPS)
    return (y * g.astype(jnp.float32) + b.astype(jnp.float32)).astype(t.dtype)

def rotary(t, positions):
    half = t.shape[-1] // 2
    inv = 1.0 / (ROPE_THETA ** (jnp.arange(half, dtype=jnp.float32) * (2.0 / t.shape[-1])))
    ang = positions.astype(jnp.float32)[:, None] * inv[None, :]
    cos, sin = jnp.cos(ang), jnp.sin(ang)
    t1, t2 = t[..., :half], t[..., half:]
    return jnp.concatenate([t1 * cos - t2 * sin, t1 * sin + t2 * cos], axis=-1)

def conformer_conv(conv_in, dw_w, dw_b, ln_g, ln_b):
    a, gate = conv_in[..., :CONV_CH], conv_in[..., CONV_CH:]
    c = a * jax.nn.sigmoid(gate)
    pad = CONV_KERNEL // 2
    c = lax.conv_general_dilated(
        c, dw_w.reshape(CONV_KERNEL, 1, CONV_CH).astype(c.dtype),
        window_strides=(1,), padding=[(pad, pad)],
        dimension_numbers=('NWC', 'WIO', 'NWC'),
        feature_group_count=CONV_CH) + dw_b.astype(c.dtype)
    c = layer_norm(c, ln_g, ln_b)
    return jax.nn.silu(c)

def dilated_branch(q, k, v, window, dilation):
    B_, H, S_, Dh = q.shape
    half = window // (2 * dilation)
    blk = half
    L = S_ // dilation
    nb = -(-L // blk)
    Lp = nb * blk
    pad = Lp - L

    def to_sub(t):
        return t.reshape(B_, H, L, dilation, Dh).transpose(0, 1, 3, 2, 4)

    qs, ks, vs = to_sub(q), to_sub(k), to_sub(v)
    qs = jnp.pad(qs, ((0, 0), (0, 0), (0, 0), (0, pad), (0, 0)))
    kp = jnp.pad(ks, ((0, 0), (0, 0), (0, 0), (blk, pad + blk), (0, 0)))
    vp = jnp.pad(vs, ((0, 0), (0, 0), (0, 0), (blk, pad + blk), (0, 0)))
    qb = qs.reshape(B_, H, dilation, nb, blk, Dh)
    kb = kp.reshape(B_, H, dilation, nb + 2, blk, Dh)
    vb = vp.reshape(B_, H, dilation, nb + 2, blk, Dh)
    kw = jnp.concatenate([kb[:, :, :, :-2], kb[:, :, :, 1:-1], kb[:, :, :, 2:]], axis=-2)
    vw = jnp.concatenate([vb[:, :, :, :-2], vb[:, :, :, 1:-1], vb[:, :, :, 2:]], axis=-2)

    qi = np.arange(nb)[:, None] * blk + np.arange(blk)[None, :]
    ki = np.arange(nb)[:, None] * blk - blk + np.arange(3 * blk)[None, :]
    valid = ((np.abs(qi[:, :, None] - ki[:, None, :]) <= half)
             & (ki[:, None, :] >= 0) & (ki[:, None, :] < L))

    s = jnp.einsum('bhrnqd,bhrnkd->bhrnqk', qb, kw) * (HEAD_DIM ** -0.5)
    s = jnp.where(jnp.asarray(valid), s, -jnp.inf)
    m = jnp.max(s, axis=-1)
    p = jnp.exp(s - m[..., None])
    den = jnp.sum(p, axis=-1)
    num = jnp.einsum('bhrnqk,bhrnkd->bhrnqd', p, vw)

    def back(t):
        tail = tuple(t.shape[5:])
        t = t.reshape((B_, H, dilation, Lp) + tail)[:, :, :, :L]
        perm = (0, 1, 3, 2) + tuple(range(4, 4 + len(tail)))
        return t.transpose(perm).reshape((B_, H, S_) + tail)

    return back(num), back(m), back(den)

def dilated_attention(q, k, v, positions):
    B_, H, S_, Dh = q.shape
    out_dtype = q.dtype
    qf = rotary(q.astype(jnp.float32), positions)
    kf = rotary(k.astype(jnp.float32), positions)
    vf = v.astype(jnp.float32)
    num_acc = den_acc = m_acc = None
    for window, dilation in DILATED_BRANCHES:
        num, m, den = dilated_branch(qf, kf, vf, window, dilation)
        if m_acc is None:
            num_acc, den_acc, m_acc = num, den, m
        else:
            m_new = jnp.maximum(m_acc, m)
            a = jnp.exp(m_acc - m_new)
            b = jnp.exp(m - m_new)
            num_acc = num_acc * a[..., None] + num * b[..., None]
            den_acc = den_acc * a + den * b
            m_acc = m_new
    o = num_acc / den_acc[..., None]
    return o.transpose(0, 2, 1, 3).reshape(B_, S_, H * Dh).astype(out_dtype)

def memory_cross_attention(h, mem_n, w_q, w_k, w_v, w_o):
    B_, S_, D = h.shape
    q = (h @ w_q).reshape(B_, S_, MEM_HEADS, MEM_HEAD_DIM)
    k = (mem_n @ w_k).reshape(B_, -1, MEM_HEADS, MEM_HEAD_DIM)
    v = (mem_n @ w_v).reshape(B_, -1, MEM_HEADS, MEM_HEAD_DIM)
    s = jnp.einsum('bshd,bmhd->bhsm', q, k, preferred_element_type=jnp.float32) * (MEM_HEAD_DIM ** -0.5)
    p = jax.nn.softmax(s, axis=-1).astype(v.dtype)
    o = jnp.einsum('bhsm,bmhd->bshd', p, v).reshape(B_, S_, D)
    return o @ w_o

def hierarchical_moe(h, w_group, b_group, w_router, b_router, w1, w3, w2):
    B_, S_, D = h.shape
    T = B_ * S_
    hf = h.reshape(T, D)
    gl = (hf @ w_group + b_group).astype(jnp.float32)
    gp = jax.nn.softmax(gl, axis=-1)
    _, g_sel = lax.top_k(gl, 1)
    g_idx = g_sel[:, 0]
    tok_idx = jnp.arange(T, dtype=jnp.int32)
    p_g = gp[tok_idx, g_idx]
    el = (hf @ w_router + b_router).astype(jnp.float32).reshape(T, N_GROUPS, EXPERTS_PER_GROUP)
    el_sel = el[tok_idx, g_idx]
    top_v, top_i = lax.top_k(el_sel, TOP_K)
    gates = p_g[:, None] * jax.nn.softmax(top_v, axis=-1)
    expert_ids = g_idx[:, None] * EXPERTS_PER_GROUP + top_i

    A = T * TOP_K
    flat_e = expert_ids.reshape(A).astype(jnp.int32)
    flat_t = jnp.repeat(tok_idx, TOP_K)
    flat_g = gates.reshape(A)
    order = jnp.argsort(flat_e)
    se, st, sg = flat_e[order], flat_t[order], flat_g[order]
    counts = jnp.bincount(flat_e, length=N_EXPERTS).astype(jnp.int32)
    starts = jnp.cumsum(counts) - counts
    pcounts = (counts + DISPATCH_BLOCK - 1) // DISPATCH_BLOCK * DISPATCH_BLOCK
    pstarts = jnp.cumsum(pcounts) - pcounts
    dest = pstarts[se] + jnp.arange(A, dtype=jnp.int32) - starts[se]
    P = (-(-A // DISPATCH_BLOCK) + N_EXPERTS) * DISPATCH_BLOCK
    n_blk = P // DISPATCH_BLOCK
    row_tok = jnp.full((P,), T, dtype=jnp.int32).at[dest].set(st)
    row_gate = jnp.zeros((P,), jnp.float32).at[dest].set(sg)
    blk_e = jnp.minimum(
        jnp.searchsorted(pstarts + pcounts, jnp.arange(n_blk, dtype=jnp.int32) * DISPATCH_BLOCK,
                         side='right'),
        N_EXPERTS - 1).astype(jnp.int32)
    x_rows = jnp.concatenate([hf, jnp.zeros((1, D), hf.dtype)], axis=0)[row_tok]
    x_blocks = x_rows.reshape(n_blk, DISPATCH_BLOCK, D)

    def expert_block(args):
        xb, e = args
        return (jax.nn.silu(xb @ w1[e]) * (xb @ w3[e])) @ w2[e]

    y_rows = lax.map(expert_block, (x_blocks, blk_e)).reshape(P, D)
    y = jax.ops.segment_sum(y_rows * row_gate[:, None].astype(y_rows.dtype), row_tok,
                            num_segments=T + 1)[:T]
    return y.reshape(B_, S_, D)

def first_inputs(seed: int = 0) -> dict:
    key = jax.random.key(seed)
    ks = jax.random.split(key, 26)
    f32 = jnp.float32
    D = D_MODEL

    def nrm(k, shape, scale):
        return jax.random.normal(k, shape, f32) * scale

    def gain(k, shape):
        return 1.0 + 0.02 * jax.random.normal(k, shape, f32)

    return {
        'x': jax.random.normal(ks[0], (BATCH, SEQ, D), f32),
        'mem': jax.random.normal(ks[1], (BATCH, MEM_LEN, D), f32),
        'positions': jnp.arange(SEQ, dtype=jnp.int32),
        'mix_norm_g': gain(ks[2], (DEPTH, D)),
        'w_in': nrm(ks[3], (DEPTH, D, IN_WIDTH), D ** -0.5),
        'conv_dw_w': nrm(ks[4], (DEPTH, CONV_KERNEL, CONV_CH), CONV_KERNEL ** -0.5),
        'conv_dw_b': nrm(ks[5], (DEPTH, CONV_CH), 0.02),
        'conv_ln_g': gain(ks[6], (DEPTH, CONV_CH)),
        'conv_ln_b': nrm(ks[7], (DEPTH, CONV_CH), 0.02),
        'conv_out_g': gain(ks[8], (DEPTH, CONV_CH)),
        'attn_out_g': gain(ks[9], (DEPTH, ATTN_WIDTH)),
        'w_out': nrm(ks[10], (DEPTH, MIX_WIDTH, D), MIX_WIDTH ** -0.5),
        'xattn_norm_g': gain(ks[11], (DEPTH, D)),
        'mem_norm_g': gain(ks[12], (DEPTH, D)),
        'w_xq': nrm(ks[13], (DEPTH, D, D), D ** -0.5),
        'w_xk': nrm(ks[14], (DEPTH, D, D), D ** -0.5),
        'w_xv': nrm(ks[15], (DEPTH, D, D), D ** -0.5),
        'w_xo': nrm(ks[16], (DEPTH, D, D), D ** -0.5),
        'moe_norm_g': gain(ks[17], (DEPTH, D)),
        'w_group': nrm(ks[18], (DEPTH, D, N_GROUPS), D ** -0.5),
        'b_group': nrm(ks[19], (DEPTH, N_GROUPS), 0.01),
        'w_router': nrm(ks[20], (DEPTH, D, N_EXPERTS), D ** -0.5),
        'b_router': nrm(ks[21], (DEPTH, N_EXPERTS), 0.01),
        'w1': nrm(ks[22], (DEPTH, N_EXPERTS, D, EXPERT_FF), D ** -0.5),
        'w3': nrm(ks[23], (DEPTH, N_EXPERTS, D, EXPERT_FF), D ** -0.5),
        'w2': nrm(ks[24], (DEPTH, N_EXPERTS, EXPERT_FF, D), EXPERT_FF ** -0.5),
        'final_norm_g': gain(ks[25], (D,)),
    }

def first_block(x, mem, positions, mix_norm_g, w_in, conv_dw_w, conv_dw_b, conv_ln_g, conv_ln_b,
              conv_out_g, attn_out_g, w_out, xattn_norm_g, mem_norm_g, w_xq, w_xk, w_xv, w_xo,
              moe_norm_g, w_group, b_group, w_router, b_router, w1, w3, w2, final_norm_g):
    B_, S_, _ = x.shape
    for l in range(DEPTH):
        h = rms_norm(x, mix_norm_g[l])
        u = h @ w_in[l]
        conv_in = u[..., :2 * CONV_CH]
        qkv = u[..., 2 * CONV_CH:].reshape(B_, S_, 3, ATTN_HEADS, HEAD_DIM).transpose(2, 0, 3, 1, 4)
        c = conformer_conv(conv_in, conv_dw_w[l], conv_dw_b[l], conv_ln_g[l], conv_ln_b[l])
        a = dilated_attention(qkv[0], qkv[1], qkv[2], positions)
        mixed = jnp.concatenate([rms_norm(c, conv_out_g[l]), rms_norm(a, attn_out_g[l])], axis=-1)
        x = x + mixed @ w_out[l]
        h = rms_norm(x, xattn_norm_g[l])
        m = rms_norm(mem, mem_norm_g[l])
        x = x + memory_cross_attention(h, m, w_xq[l], w_xk[l], w_xv[l], w_xo[l])
        h = rms_norm(x, moe_norm_g[l])
        x = x + hierarchical_moe(h, w_group[l], b_group[l], w_router[l], b_router[l], w1[l], w3[l], w2[l])
    return rms_norm(x, final_norm_g)


N_HEADS_ATTN = 8
D_ATTN = N_HEADS_ATTN * HEAD_DIM
Q_BLOCK = 128
D_SSM = D_MODEL // 2
SSM_GROUP = 16
N_SSM_GROUPS = D_SSM // SSM_GROUP
SSM_STATE = 64
DT_MIN = 1e-3
DT_MAX = 1e-1
N_EXPERT_GROUPS = 4
N_EXPERTS_2 = N_EXPERT_GROUPS * EXPERTS_PER_GROUP
D_EXPERT = D_MODEL // 4
D_IN_PROJ = 3 * D_ATTN + N_HEADS_ATTN + D_SSM + 2 * D_MODEL
EPS = 1e-6
NEG_INF = -1e30


def _rmsnorm(x, g):
    xf = x.astype(jnp.float32)
    y = xf * lax.rsqrt(jnp.mean(xf * xf, axis=-1, keepdims=True) + EPS)
    return (y * g.astype(jnp.float32)).astype(x.dtype)

def _forgetting_attention(q, k, v, f_logit):
    b, s, h, d = q.shape
    n_blk = s // Q_BLOCK
    log_f = jax.nn.log_sigmoid(f_logit.astype(jnp.float32))
    cum = jnp.cumsum(log_f, axis=1).transpose(0, 2, 1)
    qf = q.astype(jnp.float32).transpose(0, 2, 1, 3) * (d ** -0.5)
    kf = k.astype(jnp.float32).transpose(0, 2, 1, 3)
    vf = v.astype(jnp.float32).transpose(0, 2, 1, 3)
    q_blk = qf.reshape(b, h, n_blk, Q_BLOCK, d).transpose(2, 0, 1, 3, 4)
    c_blk = cum.reshape(b, h, n_blk, Q_BLOCK).transpose(2, 0, 1, 3)
    pos = jnp.arange(s, dtype=jnp.int32)
    p_blk = pos.reshape(n_blk, Q_BLOCK)

    def one_block(args):
        qb, cb, pb = args
        logits = jnp.einsum('bhqd,bhkd->bhqk', qb, kf) + cb[..., :, None] - cum[:, :, None, :]
        causal = pos[None, :] <= pb[:, None]
        logits = jnp.where(causal, logits, NEG_INF)
        p = jax.nn.softmax(logits, axis=-1)
        return jnp.einsum('bhqk,bhkd->bhqd', p, vf)

    o = lax.map(one_block, (q_blk, c_blk, p_blk))
    return o.transpose(1, 0, 3, 2, 4).reshape(b, s, h, d).astype(v.dtype)

def _linear_combine(a, b):
    a1, b1 = a
    a2, b2 = b
    return a2 * a1, a2 * b1 + b2

def _s5(u, A_re, A_im, log_dt, B_re, B_im, C_re, C_im, D_skip, w_glu):
    f32 = jnp.float32
    b, s, _ = u.shape
    uf = u.astype(f32).reshape(b, s, N_SSM_GROUPS, SSM_GROUP)
    A = lax.complex(A_re.astype(f32), A_im.astype(f32))
    dt = jnp.exp(log_dt.astype(f32))[:, None]
    A_bar = jnp.exp(A * dt)
    Bm = lax.complex(B_re.astype(f32), B_im.astype(f32))
    B_bar = ((A_bar - 1.0) / A)[..., None] * Bm
    Bu = jnp.einsum('bsgc,gpc->bsgp', uf.astype(jnp.complex64), B_bar)
    A_seq = jnp.broadcast_to(A_bar, Bu.shape)
    _, state = lax.associative_scan(_linear_combine, (A_seq, Bu), axis=1)
    Cm = lax.complex(C_re.astype(f32), C_im.astype(f32))
    y = jnp.real(jnp.einsum('gcp,bsgp->bsgc', Cm, state))
    y = y + D_skip.astype(f32).reshape(N_SSM_GROUPS, SSM_GROUP) * uf
    y = jax.nn.gelu(y.reshape(b, s, D_SSM))
    y = y * jax.nn.sigmoid(y @ w_glu.astype(f32))
    return y.astype(u.dtype)

def _hier_moe(x, w_rg, b_rg, w_re, b_re, w_gate, w_up, w_down):
    f32 = jnp.float32
    b, s, d = x.shape
    t = b * s
    xt = x.reshape(t, d)
    g_prob = jax.nn.softmax((xt @ w_rg).astype(f32) + b_rg.astype(f32), axis=-1)
    g_top, g_sel = lax.top_k(g_prob, 1)
    e_logits = ((xt @ w_re).astype(f32) + b_re.astype(f32)).reshape(t, N_EXPERT_GROUPS, EXPERTS_PER_GROUP)
    idx = jnp.broadcast_to(g_sel[:, :, None], (t, 1, EXPERTS_PER_GROUP))
    e_in = jnp.take_along_axis(e_logits, idx, axis=1)[:, 0]
    e_prob = jax.nn.softmax(e_in, axis=-1)
    e_top, e_idx = lax.top_k(e_prob, TOP_K)
    w = g_top * e_top / jnp.sum(e_top, axis=-1, keepdims=True)
    expert_id = g_sel * EXPERTS_PER_GROUP + e_idx
    combine = jnp.sum(jax.nn.one_hot(expert_id, N_EXPERTS_2, dtype=f32) * w[..., None], axis=1).astype(x.dtype)
    y = jnp.zeros_like(xt)
    for e in range(N_EXPERTS_2):
        h = jax.nn.silu(xt @ w_gate[e]) * (xt @ w_up[e])
        y = y + combine[:, e:e + 1] * (h @ w_down[e])
    return y.reshape(b, s, d)

def second_inputs(seed: int = 0) -> dict:
    key = jax.random.key(seed)
    ks = jax.random.split(key, 32)
    f32 = jnp.float32
    nrm = lambda k, shape, scale: (jax.random.normal(k, shape, f32) * scale)
    L = DEPTH
    x = jax.random.normal(ks[0], (BATCH, SEQ, D_MODEL), f32)
    norm_mix_g = 1.0 + nrm(ks[1], (L, D_MODEL), 0.02)
    w_in = nrm(ks[2], (L, D_MODEL, D_IN_PROJ), D_MODEL ** -0.5)
    b_forget = jnp.broadcast_to(jnp.linspace(1.0, 6.0, N_HEADS_ATTN, dtype=f32), (L, N_HEADS_ATTN)) + nrm(ks[3], (L, N_HEADS_ATTN), 0.1)
    q_norm_g = 1.0 + nrm(ks[4], (L, HEAD_DIM), 0.02)
    k_norm_g = 1.0 + nrm(ks[5], (L, HEAD_DIM), 0.02)
    ssm_A_re = -0.5 + nrm(ks[6], (L, N_SSM_GROUPS, SSM_STATE), 0.01)
    ssm_A_im = jnp.pi * jnp.arange(SSM_STATE, dtype=f32)[None, None, :] + nrm(ks[7], (L, N_SSM_GROUPS, SSM_STATE), 0.01)
    ssm_log_dt = jax.random.uniform(ks[8], (L, N_SSM_GROUPS), f32, math.log(DT_MIN), math.log(DT_MAX))
    ssm_B_re = nrm(ks[9], (L, N_SSM_GROUPS, SSM_STATE, SSM_GROUP), (2 * SSM_GROUP) ** -0.5)
    ssm_B_im = nrm(ks[10], (L, N_SSM_GROUPS, SSM_STATE, SSM_GROUP), (2 * SSM_GROUP) ** -0.5)
    ssm_C_re = nrm(ks[11], (L, N_SSM_GROUPS, SSM_GROUP, SSM_STATE), (2 * SSM_STATE) ** -0.5)
    ssm_C_im = nrm(ks[12], (L, N_SSM_GROUPS, SSM_GROUP, SSM_STATE), (2 * SSM_STATE) ** -0.5)
    ssm_D = nrm(ks[13], (L, D_SSM), 1.0)
    w_glu = nrm(ks[14], (L, D_SSM, D_SSM), D_SSM ** -0.5)
    w_proj_attn = nrm(ks[15], (L, D_ATTN, D_MODEL), D_ATTN ** -0.5)
    w_proj_ssm = nrm(ks[16], (L, D_SSM, D_MODEL), D_SSM ** -0.5)
    w_out = nrm(ks[17], (L, D_MODEL, D_MODEL), D_MODEL ** -0.5)
    norm_ffn_g = 1.0 + nrm(ks[18], (L, D_MODEL), 0.02)
    w_router_group = nrm(ks[19], (L, D_MODEL, N_EXPERT_GROUPS), D_MODEL ** -0.5)
    b_router_group = nrm(ks[20], (L, N_EXPERT_GROUPS), 0.01)
    w_router_expert = nrm(ks[21], (L, D_MODEL, N_EXPERTS_2), D_MODEL ** -0.5)
    b_router_expert = nrm(ks[22], (L, N_EXPERTS_2), 0.01)
    w_expert_gate = nrm(ks[23], (L, N_EXPERTS_2, D_MODEL, D_EXPERT), D_MODEL ** -0.5)
    w_expert_up = nrm(ks[24], (L, N_EXPERTS_2, D_MODEL, D_EXPERT), D_MODEL ** -0.5)
    w_expert_down = nrm(ks[25], (L, N_EXPERTS_2, D_EXPERT, D_MODEL), D_EXPERT ** -0.5)
    return {"x": x, "norm_mix_g": norm_mix_g, "w_in": w_in, "b_forget": b_forget,
            "q_norm_g": q_norm_g, "k_norm_g": k_norm_g,
            "ssm_A_re": ssm_A_re, "ssm_A_im": ssm_A_im, "ssm_log_dt": ssm_log_dt,
            "ssm_B_re": ssm_B_re, "ssm_B_im": ssm_B_im, "ssm_C_re": ssm_C_re, "ssm_C_im": ssm_C_im,
            "ssm_D": ssm_D, "w_glu": w_glu, "w_proj_attn": w_proj_attn, "w_proj_ssm": w_proj_ssm,
            "w_out": w_out, "norm_ffn_g": norm_ffn_g,
            "w_router_group": w_router_group, "b_router_group": b_router_group,
            "w_router_expert": w_router_expert, "b_router_expert": b_router_expert,
            "w_expert_gate": w_expert_gate, "w_expert_up": w_expert_up, "w_expert_down": w_expert_down}

def second_block(x, norm_mix_g, w_in, b_forget, q_norm_g, k_norm_g,
              ssm_A_re, ssm_A_im, ssm_log_dt, ssm_B_re, ssm_B_im, ssm_C_re, ssm_C_im,
              ssm_D, w_glu, w_proj_attn, w_proj_ssm, w_out, norm_ffn_g,
              w_router_group, b_router_group, w_router_expert, b_router_expert,
              w_expert_gate, w_expert_up, w_expert_down):
    b, s, _ = x.shape
    splits = np.cumsum([D_ATTN, D_ATTN, D_ATTN, N_HEADS_ATTN, D_SSM, D_MODEL]).tolist()
    for l in range(DEPTH):
        h = _rmsnorm(x, norm_mix_g[l])
        z = h @ w_in[l]
        q, k, v, f, u_ssm, g_attn, g_ssm = jnp.split(z, splits, axis=-1)
        q = _rmsnorm(q.reshape(b, s, N_HEADS_ATTN, HEAD_DIM), q_norm_g[l])
        k = _rmsnorm(k.reshape(b, s, N_HEADS_ATTN, HEAD_DIM), k_norm_g[l])
        v = v.reshape(b, s, N_HEADS_ATTN, HEAD_DIM)
        y_attn = _forgetting_attention(q, k, v, f + b_forget[l]).reshape(b, s, D_ATTN)
        y_ssm = _s5(u_ssm, ssm_A_re[l], ssm_A_im[l], ssm_log_dt[l], ssm_B_re[l], ssm_B_im[l],
                    ssm_C_re[l], ssm_C_im[l], ssm_D[l], w_glu[l])
        mixed = (jax.nn.sigmoid(g_attn) * (y_attn @ w_proj_attn[l])
                 + jax.nn.sigmoid(g_ssm) * (y_ssm @ w_proj_ssm[l]))
        x = x + mixed @ w_out[l]
        x = x + _hier_moe(_rmsnorm(x, norm_ffn_g[l]), w_router_group[l], b_router_group[l],
                          w_router_expert[l], b_router_expert[l],
                          w_expert_gate[l], w_expert_up[l], w_expert_down[l])
    return x


def setup_inputs(seed=0):
    out = dict(first_inputs(seed))
    for name, value in second_inputs(seed + 1).items():
        if name != "x":
            out[name + "_2"] = value
    return out


def reference(
    x, mem, positions, mix_norm_g, w_in, conv_dw_w, conv_dw_b, conv_ln_g, conv_ln_b, conv_out_g,
    attn_out_g, w_out, xattn_norm_g, mem_norm_g, w_xq, w_xk, w_xv, w_xo, moe_norm_g, w_group,
    b_group, w_router, b_router, w1, w3, w2, final_norm_g, norm_mix_g_2, w_in_2, b_forget_2,
    q_norm_g_2, k_norm_g_2, ssm_A_re_2, ssm_A_im_2, ssm_log_dt_2, ssm_B_re_2, ssm_B_im_2,
    ssm_C_re_2, ssm_C_im_2, ssm_D_2, w_glu_2, w_proj_attn_2, w_proj_ssm_2, w_out_2,
    norm_ffn_g_2, w_router_group_2, b_router_group_2, w_router_expert_2, b_router_expert_2,
    w_expert_gate_2, w_expert_up_2, w_expert_down_2,
):
    x = first_block(
        x, mem, positions, mix_norm_g, w_in, conv_dw_w, conv_dw_b, conv_ln_g, conv_ln_b,
        conv_out_g, attn_out_g, w_out, xattn_norm_g, mem_norm_g, w_xq, w_xk, w_xv, w_xo,
        moe_norm_g, w_group, b_group, w_router, b_router, w1, w3, w2, final_norm_g,
    )
    return second_block(
        x, norm_mix_g_2, w_in_2, b_forget_2, q_norm_g_2, k_norm_g_2, ssm_A_re_2, ssm_A_im_2,
        ssm_log_dt_2, ssm_B_re_2, ssm_B_im_2, ssm_C_re_2, ssm_C_im_2, ssm_D_2, w_glu_2,
        w_proj_attn_2, w_proj_ssm_2, w_out_2, norm_ffn_g_2, w_router_group_2, b_router_group_2,
        w_router_expert_2, b_router_expert_2, w_expert_gate_2, w_expert_up_2, w_expert_down_2,
    )


_drawn_inputs = setup_inputs


def setup_inputs(seed=0):
    import zlib

    import numpy as np

    out = dict(_drawn_inputs(seed))
    spreads = {}
    factors = {'xattn_norm_g': 4.065,
     'mem_norm_g': 3.891,
     'b_router': 5.224,
     'norm_mix_g_2': 3.472,
     'q_norm_g_2': 8.0,
     'k_norm_g_2': 6.496,
     'ssm_A_re_2': 64.0,
     'ssm_B_re_2': 3.155,
     'ssm_B_im_2': 3.254,
     'b_router_group_2': 28.421,
     'b_router_expert_2': 17.942,
     'b_group': 3.398,
     'norm_ffn_g_2': 5.241}
    for name, (base, spread) in spreads.items():
        noise = np.random.default_rng([zlib.crc32(name.encode()), seed]).standard_normal(out[name].shape)
        drawn = base * np.exp(spread * noise) if base else spread * noise
        out[name] = __import__('jax').numpy.asarray(drawn.astype(out[name].dtype))
    for name, factor in factors.items():
        out[name] = (out[name] * factor).astype(out[name].dtype)
    return out
```

```python
import math
from contextlib import ExitStack

import numpy as np

import concourse.bass as bass
from concourse import mybir

P = 128
F32 = mybir.dt.float32
I32 = mybir.dt.int32
ACT = mybir.ActivationFunctionType
ALU = mybir.AluOpType
AX = mybir.AxisListType.X

D = 1024
SEQ = 512
T = SEQ // P
KD = D // P
MEM = 256
MT = MEM // P
CONV = 256
TAPS = 31
HEADS = 12
AW = 768
IN1 = 2816
MEM_HEADS = 4
NE = 32
NG = 4
EG = NE // NG
SLOT = 64
NBLK = 48
NTAB = NBLK + 4
FF1 = 512
FF2 = 256
H2 = 8
SS = 16
NU = 4
CH = 128
RING = 4
EXPERT_RING = 6
WORK = 12288
EPS = 1e-6
LN_EPS = 1e-5
BIG = 1e30
TWO_PI = 2 * math.pi
ROUND = 1.5 * 2.0 ** 23

COLS = {}
_n = 0
for _name, _w in [
    ("mix_g", KD), ("xattn_g", KD), ("mem_g", KD), ("moe_g", KD), ("conv_out_g", 2), ("attn_out_g", 6),
    ("dw_b", 2), ("dw_w", 2 * TAPS), ("mix2_g", KD), ("ffn2_g", KD), ("qn_g", 1), ("kn_g", 1),
    ("ssm_d", NU), ("a_re", SS), ("a_im", SS), ("log_dt", SS), ("forget_b", 1),
    ("inv_freq", 1), ("group_of", 8), ("half", 2),
]:
    COLS[_name] = (_n, _n + _w)
    _n += _w
NCOL = _n
ROWS = {}
_n = 0
for _name, _w in [
    ("ln_g", CONV), ("ln_b", CONV), ("route_b1", NG + NE), ("route_b2", NG + NE),
    ("down_g", NG), ("down_e", NE), ("iota_slot", SLOT), ("iota_blk", NTAB + 1), ("iota_chunk", CH),
]:
    ROWS[_name] = (_n, _n + _w)
    _n += _w
NROW = _n


def split_two_pi():
    c1 = 6.28125
    c2 = float(np.float32(int((TWO_PI - c1) * 2 ** 19)) / np.float32(2 ** 19))
    return c1, c2, TWO_PI - c1 - c2


def shared_semaphores():
    shared = {}
    total = {}
    for tag, tiles in (("n1", 4), ("n4", 2), ("nm", 4), ("n5", 4), ("n6", 4), ("nf", 4), ("n7", 4), ("n9", 4)):
        for what, n in (("sumsq", tiles), ("var", 1), ("rstd", 1), ("xn", tiles), ("turned", KD)):
            if tag == "nf" and what in ("xn", "turned"):
                continue
            shared[f"{tag}_{what}"] = (f"norm_{what}", total.get(what, 0))
            total[what] = total.get(what, 0) + n
    counts = {}
    for tag, n in (("a1", HEADS * T), ("x5", MEM_HEADS * T), ("f2", 8 * T)):
        for what in ("scores", "masked", "probs", "turned", "pT", "rden", "pv", "out"):
            if tag == "x5" and what in ("masked", "rden"):
                continue
            shared[f"{tag}_{what}"] = (f"attn_{what}", counts.get(what, 0))
            counts[what] = counts.get(what, 0) + (KD if tag == "x5" and what in ("pv", "out") else n)
    for family, tags in (("sum", (("g1", 24), ("m4", 12), ("r3", 8), ("q5", 8), ("r5", 8), ("u", 4), ("glu", 4),
                                  ("fox", 12), ("mx", 32), ("r8", 8))),
                         ("out", (("g1", 24), ("m4", 12), ("fox", 12)))):
        base = 0
        for tag, n in tags:
            shared[f"{tag}_{family}"] = (f"dense_{family}", base)
            base += n
    for what, n in (("gexp", 1), ("gshift", 1), ("hmid", 16), ("logits", T), ("onehot", 1), ("ranks", 1), ("slots", 1),
                    ("table", 1), ("vexp", 1), ("vshift", 1), ("comb", 2 * T)):
        shared[f"{what}9"] = (f"{what}6", n)
    shared["wr9_in"] = ("wr6_in", 32)
    for j in range(4):
        shared[f"yg9_{j}"] = (f"yg6_{j}", 32)
    for slot in range(RING):
        shared[f"w_landed1_{slot}"] = (f"w_landed0_{slot}", 16 * 16 // RING)
    shared["w_used1"] = ("w_used0", 16)
    return shared


SHARED = shared_semaphores()


def recycled_semaphores():
    names = [f"{a}6{b}" for a in ("h", "xT", "hT", "silu", "tokcol", "y", "up", "down")
             for b in {"h": ("_sum", "_ready", "_turned"), "xT": ("_turned", "_ready"), "hT": ("_ready",),
                       "silu": ("",), "tokcol": ("",), "up": ("_0", "_1"),
                       "down": ("_0", "_1"),
                       "y": ("_ready", "_sum0", "_sum1", "_store0", "_store1", "_store2", "_store3")}[a]]
    taken = {name.replace("6", "9"): name for name in names}
    later = ("up9_2", "up9_3", "down9_2", "down9_3", "y9_sum2", "y9_sum3", "s5_added", "s5_in", "s5_in_read",
             "s5_mat_steps", "s5_mats", "s5_pad_steps", "s5_padded", "s5_prod")
    earlier = ("raw_ready", "rot_c_ready", "swapped", "swap_used", "rotated", "conv_tap", "conv_turned", "conv_done",
               "ln_var", "ln_rstd", "ln_sig", "ln_done", "angles", "sines")
    assert len(later) == len(earlier)
    taken.update(zip(later, earlier))
    return taken


RECYCLED = recycled_semaphores()


def build(nc, a, out):
    es = ExitStack()
    with es:
        def sb(name, shape, dt=F32):
            return es.enter_context(nc.sbuf_tensor(name, shape, dt))

        sems = {}

        def S(name):
            name = RECYCLED.get(name, name)
            name = SHARED.get(name, (name, 0))[0]
            if name not in sems:
                sems[name] = es.enter_context(nc.semaphore(name))
            return sems[name]

        def since(name):
            return SHARED.get(name, (name, 0))[1]

        ps = es.enter_context(nc.psum_tensor("ps", [P, 8, 512], F32))
        ring = sb("ring", [P, EXPERT_RING, KD * 512])
        spare = ring[:, RING:EXPERT_RING, :].rearrange("p a n -> p (a n)")
        x = sb("x", [P, T, D])
        hT = sb("hT", [P, KD, SEQ])
        xn = sb("xn", [P, T, D])
        work = sb("work", [P, WORK])
        cols = sb("cols", [P, NCOL])
        rows = sb("rows", [P, NROW])
        ident = sb("ident", [P, P])
        junk = sb("junk", [P, D])
        junk2 = spare[:, 0:D]
        st = sb("st", [P, 64])
        halves = sb("halves", [P, 16])

        def col(name, i=0, n=1, p0=0, p1=P):
            return cols[p0:p1, COLS[name][0] + i:COLS[name][0] + i + n]

        def row(name, p1=P):
            return rows[0:p1, ROWS[name][0]:ROWS[name][1]]

        class Area:
            def __init__(self, start=0):
                self.at = start

            def take(self, *shape):
                n = int(np.prod(shape))
                v = work[:, self.at:self.at + n]
                self.at += n
                assert self.at <= WORK, self.at
                if len(shape) == 2:
                    v = v.rearrange("p (a b) -> p a b", a=shape[0])
                if len(shape) == 3:
                    v = v.rearrange("p (a b c) -> p a b c", a=shape[0], b=shape[1])
                return v

        stage_n = {"pe": 0, "act": 0, "dve": 0, "pool": 0}
        chain_n = {"act": 0, "dve": 0, "pool": 0}

        def end_stage(name, eng):
            stage_n[name] += 1
            eng.drain().then_inc(S("stage_done"), 1)
            eng.wait_ge(S("stage_done"), 4 * stage_n[name])

        def link(name, eng, ins):
            chain_n[name] += 1
            ins.then_inc(S(f"{name}_chain"), 1)
            eng.wait_ge(S(f"{name}_chain"), since(f"{name}_chain") + chain_n[name])

        def accumulate(out_, pairs):
            for i, (l, r) in enumerate(pairs):
                last = nc.tensor.matmul(out_, l, r, start=i == 0, stop=i == len(pairs) - 1)
            return last

        chunks = []

        def dense(name, w, c0, c1):
            chunks.append((name, w, c0, c1))

        w_in = a["w_in"][0]
        for c in range(6):
            dense(f"in{c}", w_in, 512 * c, min(512 * c + 512, IN1))
        for nm in ("w_xk", "w_xv", "w_out", "w_xq", "w_xo"):
            for c in range(2):
                dense(f"{nm}{c}", a[nm][0], 512 * c, 512 * c + 512)
        n_first = len(chunks)
        w2i = a["w_in_2"][0]
        dense("u", w2i, 1544, 2056)
        dense("glu", a["w_glu_2"][0], 0, 512)
        for nm, c0 in (("q", 0), ("k", 512), ("v", 1024)):
            dense(nm, w2i, c0, c0 + 512)
        for c in range(2):
            dense(f"ga{c}", w2i, 2056 + 512 * c, 2568 + 512 * c)
            dense(f"gs{c}", w2i, 3080 + 512 * c, 3592 + 512 * c)
            dense(f"pa{c}", a["w_proj_attn_2"][0], 512 * c, 512 * c + 512)
            dense(f"ps{c}", a["w_proj_ssm_2"][0], 512 * c, 512 * c + 512)
        for c in range(2):
            dense(f"w_out_2{c}", a["w_out_2"][0], 512 * c, 512 * c + 512)
        place = {}
        for i, (nm, w, c0, c1) in enumerate(chunks):
            part = i >= n_first
            j = i - n_first if part else i
            place[nm] = (part, j, j % RING, w.shape[0] // P, c1 - c0)

        def weight(nm):
            _, _, slot, kt, w = place[nm]
            return ring[:, slot, 0:kt * w].rearrange("p (k n) -> p k n", k=kt)

        def arrived(pe, nm):
            part, j, slot, _, _ = place[nm]
            pe.wait_ge(S(f"w_landed{int(part)}_{slot}"), since(f"w_landed{int(part)}_{slot}") + 16 * (j // RING + 1))

        def load_part(sp, part):
            for i, (nm, w, c0, c1) in enumerate(chunks):
                if (i >= n_first) != part:
                    continue
                _, j, slot, _, _ = place[nm]
                if j >= RING:
                    sp.wait_ge(S(f"w_used{int(part)}"), since(f"w_used{int(part)}") + j - RING + 1)
                sp.dma_start(weight(nm), w[:, c0:c1].rearrange("(k p) n -> p k n", p=P)).then_inc(
                    S(f"w_landed{int(part)}_{slot}"), 16)

        def w_used(part, ins):
            ins.then_inc(S(f"w_used{part}"), 1)

        def norm_act(tag, src, width, tiles, dst, gain, at=0, eps=EPS):
            for t in range(tiles):
                nc.scalar.activation(junk[:, 0:width], src(t), ACT.Square,
                                     accum_out=st[:, at + t:at + t + 1]).then_inc(S(tag + "_sumsq"), 1)
                nc.scalar.wait_ge(S(tag + "_sumsq"), since(tag + "_sumsq") + t + 1)
            transposed_act(tag, dst, gain)

        def transposed_act(tag, dst, gain, n=KD):
            for k in range(0, n, 2):
                nc.scalar.wait_ge(S(tag + "_turned"), since(tag + "_turned") + k + 1)
                nc.scalar.activation(dst(k), ps[:, k, 0:dst(k).shape[-1]], ACT.Identity, scale=gain(k))

        def norm_dve(tag, src, width, tiles, mid, dst, gain, at=0, eps=EPS):
            dve = nc.vector
            dve.wait_ge(S(tag + "_sumsq"), since(tag + "_sumsq") + tiles)
            dve.tensor_scalar(st[:, 8 + at:8 + at + tiles], st[:, at:at + tiles], 1.0 / width, eps,
                              ALU.mult, ALU.add).then_inc(S(tag + "_var"), 1)
            dve.wait_ge(S(tag + "_rstd"), since(tag + "_rstd") + 1)
            for t in range(tiles):
                dve.tensor_scalar(mid(t), src(t), st[:, 16 + at + t:17 + at + t], None,
                                  ALU.mult).then_inc(S(tag + "_xn"), 1)
            transposed_dve(tag, dst, gain)

        def transposed_dve(tag, dst, gain, n=KD):
            for k in range(1, n, 2):
                nc.vector.wait_ge(S(tag + "_turned"), since(tag + "_turned") + k + 1)
                nc.vector.tensor_scalar(dst(k), ps[:, k, 0:dst(k).shape[-1]], gain(k), None, ALU.mult)

        def norm_pool(tag, tiles, at=0):
            nc.gpsimd.wait_ge(S(tag + "_var"), since(tag + "_var") + 1)
            nc.gpsimd.tensor_tensor(st[:, 16 + at:16 + at + tiles], st[:, 8 + at:8 + at + tiles],
                                    halves[:, 0:tiles], ALU.pow).then_inc(S(tag + "_rstd"), 1)

        def norm_pe(tag, mid, tiles, n=KD):
            for k in range(n):
                for t in range(tiles):
                    if k == 0:
                        nc.tensor.wait_ge(S(tag + "_xn"), since(tag + "_xn") + t + 1)
                    last = nc.tensor.transpose(ps[:, k, t * P:t * P + P], mid(t)[:, k * P:k * P + P], ident[:, :])
                last.then_inc(S(tag + "_turned"), 1)

        def x_tile(t):
            return x[:, t, :]

        def xn_tile(t):
            return xn[:, t, :]

        def hT_tile(k):
            return hT[:, k, :]

        def gains(name):
            return lambda k: col(name, k)

        def residual_pe(tag, src, names, part):
            for n, nm in enumerate(names):
                arrived(nc.tensor, nm)
                for t in range(T):
                    last = accumulate(ps[:, n * T + t, :],
                                      [(src(k)[:, t * P:t * P + P], weight(nm)[:, k, :]) for k in range(KD)])
                    last.then_inc(S(tag + "_sum"), 1)
                nc.tensor.wait_ge(S(tag + "_sum"), since(tag + "_sum") + T * (n + 1))
                nc.tensor.sem_inc(S(f"w_used{part}"), 1)

        def residual_dve(tag):
            for n in range(2):
                for t in range(T):
                    nc.vector.wait_ge(S(tag + "_sum"), since(tag + "_sum") + n * T + t + 1)
                    xs = x[:, t, n * 512:n * 512 + 512]
                    nc.vector.tensor_tensor(xs, xs, ps[:, n * T + t, :], ALU.add)

        A1 = Area()
        v1 = A1.take(T, AW)
        k1 = A1.take(6, SEQ)
        q1 = A1.take(HEADS, SEQ)
        assert A1.at == 3072 + 3072 + 6144
        o1 = lambda t: xn[:, t, 0:AW]
        ctok = spare[:, 1024:2048].rearrange("p (t n) -> p t n", t=T)
        big1 = spare[:, 2048:4156]
        cpad = big1[:, 0:1084].rearrange("p (c n) -> p c n", c=2)
        cacc = big1[:, 1084:2108].rearrange("p (c n) -> p c n", c=2)
        mask1 = spare[:, 6208:6208 + 3 * P + SEQ]

        cos_t, sin_t = xn[:, 0, 0:SEQ], xn[:, 0, SEQ:D]
        perm = xn[:, 3, 0:P]
        posf, ang, turns = xn[:, 1, 0:SEQ], xn[:, 1, SEQ:D], xn[:, 2, 0:SEQ]
        raw = lambda f: junk2[:, (f % 2) * 512:(f % 2) * 512 + 512]
        rot_c = lambda f: big2[:, f % 2, 0:512]
        rot_s = lambda f: big2[:, f % 2, 512:1024]
        big2 = spare[:, 4160:6208].rearrange("p (a n) -> p a n", a=2)
        posi = spare[:, 7168:7680].bitcast(I32)

        def sin_cos_dve(dve, src, n_turn, c_out, s_out, cosine):
            def L(i):
                link("dve", dve, i)
            L(dve.tensor_scalar(n_turn, src, 1.0 / TWO_PI, ROUND, ALU.mult, ALU.add))
            L(dve.tensor_scalar(n_turn, n_turn, -ROUND, None, ALU.add))
            for c in split_two_pi():
                L(dve.scalar_tensor_tensor(src, n_turn, -c, src, ALU.mult, ALU.add))
            L(dve.tensor_scalar(s_out, src, -math.pi, math.pi, ALU.max, ALU.min))
            L(dve.tensor_scalar(n_turn, src, math.pi / 2, -TWO_PI, ALU.is_gt, ALU.mult))
            L(dve.scalar_tensor_tensor(c_out, src, math.pi / 2, n_turn, ALU.add, ALU.add))
            L(dve.tensor_scalar(c_out, c_out, -math.pi, math.pi, ALU.max, ALU.min))

        block = es.enter_context(nc.Block())
        FT = [2, 3, 0, 1] + list(range(4, 16))
        QK0 = 4

        def stage1_pe(pe):
            norm_pe("n1", xn_tile, T)
            end_stage("pe", pe)
            used = 0
            for g in range(16 + 2):
                if g < 16:
                    f = FT[g]
                    if g == 0:
                        arrived(pe, "in0")
                    elif f % 4 == 0:
                        arrived(pe, f"in{f // 4}")
                    if g >= 6:
                        pe.wait_ge(S("g1_out"), since("g1_out") + g - 5)
                    wv = weight(f"in{f // 4}")
                    last = accumulate(ps[:, g % 6, :], [(wv[:, k, (f % 4) * P:(f % 4) * P + P], hT[:, k, :])
                                                        for k in range(KD)])
                    last.then_inc(S("g1_sum"), 1)
                    if g in (3, 7, 11, 15):
                        pe.wait_ge(S("g1_sum"), since("g1_sum") + g + 1)
                        pe.sem_inc(S("w_used0"), 1)
                f = g - 2 - QK0
                if f >= 0:
                    pe.wait_ge(S("raw_ready"), f + 1)
                    if f >= 2:
                        pe.wait_ge(S("swap_used"), f - 1)
                    if f == 0:
                        pe.wait_ge(S("perm_in"), 16)
                    nc.tensor.matmul(ps[:, 6 + f % 2, :], perm, raw(f), start=True, stop=True).then_inc(
                        S("swapped"), 1)
            for c, w in ((4, 512), (5, 256)):
                arrived(pe, f"in{c}")
                for t in range(T):
                    g = 16 + (c - 4) * T + t
                    pe.wait_ge(S("g1_out"), since("g1_out") + g - 5)
                    last = accumulate(ps[:, g % 6, 0:w], [(hT[:, k, t * P:t * P + P], weight(f"in{c}")[:, k, :])
                                                          for k in range(KD)])
                    last.then_inc(S("g1_sum"), 1)
                pe.wait_ge(S("g1_sum"), since("g1_sum") + 16 + T * (c - 3))
                pe.sem_inc(S("w_used0"), 1)
            pe.wait_ge(S("conv_done"), 2)
            pe.wait_ge(S("swap_used"), 12)
            for t in range(T):
                for c in range(2):
                    last = nc.tensor.transpose(ps[:, 6 + t // 2, (t % 2) * 256 + c * P:(t % 2) * 256 + c * P + P],
                                               cacc[:, c, t * P:t * P + P], ident[:, :])
            last.then_inc(S("conv_turned"), 1)
            end_stage("pe", pe)

        def stage1_act(act):
            act.wait_ge(S("x_in"), 16)
            act.wait_ge(S("par_in"), 16 * 7)
            norm_act("n1", x_tile, D, T, hT_tile, gains("mix_g"))
            end_stage("act", act)
            act.dma_start(perm, a["perm"]).then_inc(S("perm_in"), 16)
            act.wait_ge(S("angles"), 1)
            nc.scalar.activation(sin_t, sin_t, ACT.Sin)
            nc.scalar.activation(cos_t, cos_t, ACT.Sin).then_inc(S("sines"), 1)
            for g in range(24):
                act.wait_ge(S("g1_sum"), since("g1_sum") + g + 1)
                if g < 2:
                    nc.scalar.activation(big2[:, 0, g * 512:g * 512 + 512], ps[:, g, :], ACT.Sigmoid).then_inc(
                        S("g1_out"), 1)
                elif g < 4:
                    continue
                elif g < 16:
                    f = g - 4
                    if f >= 2:
                        act.wait_ge(S("rot_c_ready"), f - 1)
                        act.wait_ge(S("swapped"), f - 1)
                    if g == 4:
                        act.wait_ge(S("g1_out"), since("g1_out") + 4)
                    nc.scalar.copy(raw(f), ps[:, g % 6, :]).then_inc(S("raw_ready"), 1)
                    act.wait_ge(S("raw_ready"), f + 1)
                    act.sem_inc(S("g1_out"), 1)
                else:
                    t, c = (g - 16) % T, (g - 16) // T
                    w = 512 if c == 0 else 256
                    nc.scalar.copy(v1[:, t, c * 512:c * 512 + w], ps[:, g % 6, 0:w]).then_inc(S("g1_out"), 1)
            act.wait_ge(S("conv_turned"), 1)
            nc.scalar.copy(ctok[:, 0:2, :], ps[:, 6, :].rearrange("p (t n) -> p t n", t=2))
            nc.scalar.copy(ctok[:, 2:4, :], ps[:, 7, :].rearrange("p (t n) -> p t n", t=2)).then_inc(S("ctok_in"), 1)
            act.wait_ge(S("ln_done"), 1)
            nc.scalar.activation(junk2[:, 0:1024], ctok[:, :, :].rearrange("p t n -> p (t n)"),
                                 ACT.Sigmoid).then_inc(S("ln_sig"), 1)
            end_stage("act", act)

        def stage1_dve(dve):
            def L(i):
                link("dve", dve, i)
            dve.memset(halves[:, :], -0.5)
            L(dve.memset(big1[:, :], 0.0))
            L(dve.memset(work[:, 6144:6144 + 6144], 0.0))
            dve.wait_ge(S("x_in"), 16)
            dve.wait_ge(S("par_in"), 16 * 7)
            norm_dve("n1", x_tile, D, T, xn_tile, hT_tile, gains("mix_g"))
            end_stage("dve", dve)
            L(dve.tensor_copy(posf, posi[:, :]))
            L(dve.tensor_scalar(ang, posf, col("inv_freq"), None, ALU.mult))
            sin_cos_dve(dve, ang, turns, cos_t, sin_t, True)
            dve.drain().then_inc(S("angles"), 1)
            for c in range(2):
                dve.wait_ge(S("g1_out"), since("g1_out") + 2)
                dve.wait_ge(S("g1_sum"), since("g1_sum") + 3 + c)
                L(dve.tensor_tensor(cpad[:, c, 15:15 + SEQ], ps[:, 2 + c, :], big2[:, 0, c * 512:c * 512 + 512], ALU.mult))
                dve.sem_inc(S("g1_out"), 1)
            taps = [0]

            def conv_step():
                j = taps[0]
                if j >= TAPS:
                    return
                taps[0] += 1
                for c in range(2):
                    w = col("dw_w", c * TAPS + j)
                    if j == 0:
                        ins = dve.tensor_scalar(cacc[:, c, :], cpad[:, c, 0:SEQ], w, col("dw_b", c), ALU.mult, ALU.add)
                    else:
                        ins = dve.scalar_tensor_tensor(cacc[:, c, :], cpad[:, c, j:j + SEQ], w, cacc[:, c, :],
                                                       ALU.mult, ALU.add)
                    if j == TAPS - 1:
                        ins.then_inc(S("conv_done"), 1)
                    else:
                        ins.then_inc(S("conv_tap"), 1)
                if j < TAPS - 1:
                    dve.wait_ge(S("conv_tap"), 2 * (j + 1))

            dve.wait_ge(S("sines"), 1)
            for f in range(12):
                scale = HEAD_SCALE if f < 6 else 1.0
                dve.wait_ge(S("raw_ready"), f + 1)
                if f >= 2:
                    dve.wait_ge(S("rotated"), ROT(f - 2))
                dve.scalar_tensor_tensor(rot_c(f), raw(f), scale, cos_t, ALU.mult, ALU.mult).then_inc(S("rot_c_ready"), 1)
                dve.wait_ge(S("swapped"), f + 1)
                dve.scalar_tensor_tensor(rot_s(f), ps[:, 6 + f % 2, :], scale, sin_t, ALU.mult, ALU.mult).then_inc(
                    S("swap_used"), 1)
                conv_step()
                conv_step()
            while taps[0] < TAPS:
                conv_step()
            dve.wait_ge(S("ctok_in"), 1)
            bc = lambda v: v.unsqueeze(2).to_broadcast([P, T, CONV])
            rb = lambda nm: row(nm).unsqueeze(1).to_broadcast([P, T, CONV])
            jv = junk2[:, :].rearrange("p (t n) -> p t n", t=T)
            L(dve.tensor_reduce(st[:, 24:28], ctok[:, :, :], AX, ALU.add))
            L(dve.tensor_scalar(st[:, 28:32], st[:, 24:28], -1.0 / CONV, None, ALU.mult))
            L(dve.tensor_tensor(ctok[:, :, :], ctok[:, :, :], bc(st[:, 28:32]), ALU.add))
            L(dve.tensor_tensor(jv, ctok[:, :, :], ctok[:, :, :], ALU.mult))
            L(dve.tensor_reduce(st[:, 24:28], jv, AX, ALU.add))
            dve.tensor_scalar(st[:, 32:36], st[:, 24:28], 1.0 / CONV, LN_EPS, ALU.mult, ALU.add).then_inc(S("ln_var"), 1)
            dve.wait_ge(S("ln_rstd"), 1)
            L(dve.tensor_tensor(ctok[:, :, :], ctok[:, :, :], bc(st[:, 36:40]), ALU.mult))
            L(dve.tensor_tensor(ctok[:, :, :], ctok[:, :, :], rb("ln_g"), ALU.mult))
            dve.tensor_tensor(ctok[:, :, :], ctok[:, :, :], rb("ln_b"), ALU.add).then_inc(S("ln_done"), 1)
            dve.wait_ge(S("ln_sig"), 1)
            L(dve.tensor_tensor(ctok[:, :, :], ctok[:, :, :], jv, ALU.mult))
            L(dve.tensor_tensor(jv, ctok[:, :, :], ctok[:, :, :], ALU.mult))
            L(dve.tensor_reduce(st[:, 24:28], jv, AX, ALU.add))
            dve.tensor_scalar(st[:, 32:36], st[:, 24:28], 1.0 / CONV, EPS, ALU.mult, ALU.add).then_inc(S("ln_var"), 1)
            dve.wait_ge(S("ln_rstd"), 2)
            L(dve.tensor_tensor(ctok[:, :, :], ctok[:, :, :], bc(st[:, 36:40]), ALU.mult))
            end_stage("dve", dve)

        HEAD_SCALE = 0.125

        def ROT(f):
            return 2 * (f + 1) if f < 6 else 12 + (f - 5)

        def stage1_pool(pool):
            norm_pool("n1", T)
            end_stage("pool", pool)
            for f in range(12):
                pool.wait_ge(S("rot_c_ready"), f + 1)
                pool.wait_ge(S("swap_used"), f + 1)
                if f < 6:
                    for hh in range(2):
                        r = slice(64 * hh, 64 * hh + 64)
                        nc.gpsimd.tensor_tensor(q1[r, 2 * f + hh, :], big2[r, f % 2, 0:512], big2[r, f % 2, 512:1024],
                                                ALU.add).then_inc(S("rotated"), 1)
                else:
                    nc.gpsimd.tensor_tensor(k1[:, f - 6, :], rot_c(f), rot_s(f), ALU.add).then_inc(S("rotated"), 1)
                pool.wait_ge(S("rotated"), ROT(f))
            for i in range(2):
                pool.wait_ge(S("ln_var"), i + 1)
                nc.gpsimd.tensor_tensor(st[:, 36:40], st[:, 32:36], halves[:, 0:T], ALU.pow).then_inc(S("ln_rstd"), 1)
            end_stage("pool", pool)

        N1 = HEADS * T
        sm = lambda i: junk[:, (i % 2) * 512:(i % 2) * 512 + 512]
        pr = lambda i: junk2[:, (i % 2) * 512:(i % 2) * 512 + 512]
        pT = lambda i: big2[:, i % 2, 0:512]
        nmax = sb("nmax", [P, 64])
        den = sb("den", [P, 64])
        rden = sb("rden", [P, 64])

        def attn1_pe(pe):
            for i in range(N1 + 2):
                if i < N1:
                    h, t = i // T, i % T
                    if i >= 2:
                        pe.wait_ge(S("a1_masked"), since("a1_masked") + i - 1)
                    nc.tensor.matmul(ps[:, i % 2, :], q1[:, h, t * P:t * P + P], k1[:, h // 2, :],
                                     start=True, stop=True).then_inc(S("a1_scores"), 1)
                j = i - 1
                if 0 <= j < N1:
                    pe.wait_ge(S("a1_probs"), since("a1_probs") + j + 1)
                    if j >= 2:
                        pe.wait_ge(S("a1_pT"), since("a1_pT") + j - 1)
                    for c in range(4):
                        last = nc.tensor.transpose(ps[:, 2 + j % 2, c * P:c * P + P], pr(j)[:, c * P:c * P + P],
                                                   ident[:, :])
                    last.then_inc(S("a1_turned"), 1)
                j = i - 2
                if j >= 0:
                    h = j // T
                    pe.wait_ge(S("a1_pT"), since("a1_pT") + j + 1)
                    if j >= 2:
                        pe.wait_ge(S("a1_out"), since("a1_out") + j - 1)
                    accumulate(ps[:, 4 + j % 2, 0:P],
                               [(pT(j)[:, c * P:c * P + P], v1[:, c, (h // 2) * P:(h // 2) * P + P]) for c in range(4)]
                               ).then_inc(S("a1_pv"), 1)
            end_stage("pe", pe)

        def attn1_dve(dve):
            for i in range(N1 + 1):
                if i < N1:
                    t = i % T
                    dve.wait_ge(S("a1_scores"), since("a1_scores") + i + 1)
                    if i >= 2:
                        dve.wait_ge(S("a1_probs"), since("a1_probs") + i - 1)
                    m0 = 3 * P - P * t
                    dve.tensor_tensor_reduce(out=sm(i), in0=ps[:, i % 2, :], in1=mask1[:, m0:m0 + SEQ], scale=-1.0,
                                             scalar=BIG, op0=ALU.add, op1=ALU.min,
                                             accum_out=nmax[:, i:i + 1]).then_inc(S("a1_masked"), 1)
                j = i - 1
                if j >= 0:
                    dve.wait_ge(S("a1_turned"), since("a1_turned") + j + 1)
                    if j >= 2:
                        dve.wait_ge(S("a1_pv"), since("a1_pv") + j - 1)
                    dve.tensor_copy(pT(j), ps[:, 2 + j % 2, :]).then_inc(S("a1_pT"), 1)
                    dve.wait_ge(S("a1_probs"), since("a1_probs") + j + 1)
                    dve.reciprocal(rden[:, j:j + 1], den[:, j:j + 1]).then_inc(S("a1_rden"), 1)
            end_stage("dve", dve)

        def attn1_act(act):
            for i in range(N1 + 2):
                if i < N1:
                    act.wait_ge(S("a1_masked"), since("a1_masked") + i + 1)
                    if i >= 2:
                        act.wait_ge(S("a1_turned"), since("a1_turned") + i - 1)
                    nc.scalar.activation(pr(i), sm(i), ACT.Exp, bias=nmax[:, i:i + 1], scale=-1.0,
                                         accum_out=den[:, i:i + 1]).then_inc(S("a1_probs"), 1)
                j = i - 2
                if j >= 0:
                    h, t = j // T, j % T
                    act.wait_ge(S("a1_pv"), since("a1_pv") + j + 1)
                    act.wait_ge(S("a1_rden"), since("a1_rden") + j + 1)
                    nc.scalar.activation(xn[:, t, h * 64:h * 64 + 64], ps[:, 4 + j % 2, (h % 2) * 64:(h % 2) * 64 + 64],
                                         ACT.Identity, scale=rden[:, j:j + 1]).then_inc(S("a1_out"), 1)
            end_stage("act", act)

        def mix_gain(k):
            return col("conv_out_g", k) if k < 2 else col("attn_out_g", k - 2)

        def mix_pe(pe):
            for k in range(KD):
                for t in range(T):
                    if k == 2:
                        pe.wait_ge(S("nm_xn"), since("nm_xn") + t + 1)
                    src = ctok[:, t, k * P:k * P + P] if k < 2 else xn[:, t, (k - 2) * P:(k - 1) * P]
                    last = nc.tensor.transpose(ps[:, k, t * P:t * P + P], src, ident[:, :])
                last.then_inc(S("nm_turned"), 1)
            end_stage("pe", pe)

        A4 = Area()
        memx = hT[:, 0:4, :].rearrange("p (m a) n -> p m (a n)", m=MT)
        A4.take(MT, D)
        memn = A4.take(MT, D)
        memT = A4.take(KD, MEM)
        kx = A4.take(KD, MEM)
        vx = A4.take(MT, D)
        A5 = Area(kx_end := 5 * 2048)
        pxT = big1[:, 0:1024].rearrange("p (m q) -> p m q", m=MT)
        qx = work[:, 0:4096].rearrange("p (k n) -> p k n", k=KD)

        def memT_tile(k):
            return memT[:, k, :]

        def mem_pe(pe):
            norm_pe("n4", lambda t: memn[:, t, :], MT)
            end_stage("pe", pe)
            for c in range(2):
                arrived(pe, f"w_xk{c}")
                for i in range(4):
                    f = 4 * c + i
                    last = accumulate(ps[:, f, 0:MEM], [(weight(f"w_xk{c}")[:, k, i * P:i * P + P], memT[:, k, :])
                                                        for k in range(KD)])
                    last.then_inc(S("m4_sum"), 1)
                pe.wait_ge(S("m4_sum"), since("m4_sum") + 4 * (c + 1))
                pe.sem_inc(S("w_used0"), 1)
            for c in range(2):
                arrived(pe, f"w_xv{c}")
                for t in range(MT):
                    g = 8 + 2 * c + t
                    pe.wait_ge(S("m4_out"), since("m4_out") + g - 7)
                    last = accumulate(ps[:, g - 8, :], [(memT[:, k, t * P:t * P + P], weight(f"w_xv{c}")[:, k, :])
                                                        for k in range(KD)])
                    last.then_inc(S("m4_sum"), 1)
                pe.wait_ge(S("m4_sum"), since("m4_sum") + 8 + 2 * (c + 1))
                pe.sem_inc(S("w_used0"), 1)
            end_stage("pe", pe)

        def mem_act(act):
            act.wait_ge(S("zeros"), 1)
            act.dma_start(ymid.rearrange("(r p) n -> p r n", p=P),
                          zeros.unsqueeze(1).to_broadcast([P, NBLK * SLOT // P, D])).then_inc(S("ymid_zeroed"), 16)
            act.wait_ge(S("mem_in"), 16)
            norm_act("n4", lambda t: memx[:, t, :], D, MT, memT_tile, gains("mem_g"))
            end_stage("act", act)
            for g in range(12):
                act.wait_ge(S("m4_sum"), since("m4_sum") + g + 1)
                if g < 8:
                    nc.scalar.copy(kx[:, g, :], ps[:, g, 0:MEM]).then_inc(S("m4_out"), 1)
                else:
                    c, t = (g - 8) // 2, g % 2
                    nc.scalar.copy(vx[:, t, c * 512:c * 512 + 512], ps[:, g - 8, :]).then_inc(S("m4_out"), 1)
            end_stage("act", act)

        zeros = work[:, WORK - D:WORK]

        def mem_dve(dve):
            dve.memset(zeros, 0.0).then_inc(S("zeros"), 1)
            dve.wait_ge(S("mem_in"), 16)
            norm_dve("n4", lambda t: memx[:, t, :], D, MT, lambda t: memn[:, t, :], memT_tile, gains("mem_g"))
            end_stage("dve", dve)
            end_stage("dve", dve)

        def mem_pool(pool):
            norm_pool("n4", MT)
            end_stage("pool", pool)
            end_stage("pool", pool)

        NX = MEM_HEADS * T
        XSCALE = (D // MEM_HEADS) ** -0.5

        def xattn_pe(pe):
            norm_pe("n5", xn_tile, T)
            end_stage("pe", pe)
            for c in range(2):
                arrived(pe, f"w_xq{c}")
                for i in range(4):
                    last = accumulate(ps[:, 4 * c + i, :], [(weight(f"w_xq{c}")[:, k, i * P:i * P + P], hT[:, k, :])
                                                            for k in range(KD)])
                    last.then_inc(S("q5_sum"), 1)
                pe.wait_ge(S("q5_sum"), since("q5_sum") + 4 * (c + 1))
                pe.sem_inc(S("w_used0"), 1)
            end_stage("pe", pe)
            for i in range(NX + 2):
                if i < NX:
                    h, t = i // T, i % T
                    if i >= 2:
                        pe.wait_ge(S("x5_probs"), since("x5_probs") + i - 1)
                    accumulate(ps[:, i % 2, 0:MEM], [(qx[:, 2 * h + e, t * P:t * P + P], kx[:, 2 * h + e, :])
                                                     for e in range(2)]).then_inc(S("x5_scores"), 1)
                j = i - 1
                if 0 <= j < NX:
                    pe.wait_ge(S("x5_norm"), j + 1)
                    if j >= 2:
                        pe.wait_ge(S("x5_pT"), since("x5_pT") + j - 1)
                    for m in range(MT):
                        last = nc.tensor.transpose(ps[:, 2 + j % 2, m * P:m * P + P], pr(j)[:, m * P:m * P + P], ident[:, :])
                    last.then_inc(S("x5_turned"), 1)
                if j >= 0 and j % T == T - 1:
                    h = j // T
                    pe.wait_ge(S("x5_pT"), since("x5_pT") + j + 1)
                    for e in range(2):
                        if h >= 1:
                            pe.wait_ge(S("x5_out"), since("x5_out") + 2 * h - 1 + e)
                        accumulate(ps[:, 4 + e, :], [(vx[:, m, (2 * h + e) * P:(2 * h + e + 1) * P], pxT[:, m, :])
                                                     for m in range(MT)]).then_inc(S("x5_pv"), 1)
            end_stage("pe", pe)
            residual_pe("r5", lambda k: hT[:, k, :], ["w_xo0", "w_xo1"], 0)
            end_stage("pe", pe)

        def xattn_act(act):
            norm_act("n5", x_tile, D, T, hT_tile, gains("xattn_g"))
            end_stage("act", act)
            for f in range(KD):
                act.wait_ge(S("q5_sum"), since("q5_sum") + f + 1)
                nc.scalar.mul(qx[:, f, :], ps[:, f, :], XSCALE)
            end_stage("act", act)
            for i in range(NX + 1):
                if i < NX:
                    act.wait_ge(S("x5_max"), i + 1)
                    if i >= 2:
                        act.wait_ge(S("x5_turned"), since("x5_turned") + i - 1)
                    nc.scalar.activation(pr(i)[:, 0:MEM], ps[:, i % 2, 0:MEM], ACT.Exp, bias=nmax[:, i:i + 1],
                                         accum_out=den[:, i:i + 1]).then_inc(S("x5_probs"), 1)
                if i >= 1 and i % T == 0:
                    h = i // T - 1
                    for e in range(2):
                        act.wait_ge(S("x5_pv"), since("x5_pv") + 2 * h + e + 1)
                        nc.scalar.copy(hT[:, 2 * h + e, :], ps[:, 4 + e, :]).then_inc(S("x5_out"), 1)
            end_stage("act", act)
            end_stage("act", act)

        def xattn_dve(dve):
            norm_dve("n5", x_tile, D, T, xn_tile, hT_tile, gains("xattn_g"))
            end_stage("dve", dve)
            end_stage("dve", dve)
            for i in range(NX + 1):
                if i < NX:
                    dve.wait_ge(S("x5_scores"), since("x5_scores") + i + 1)
                    dve.tensor_reduce(rden[:, i:i + 1], ps[:, i % 2, 0:MEM], AX, ALU.max).then_inc(S("x5_rmax"), 1)
                    dve.wait_ge(S("x5_rmax"), i + 1)
                    dve.tensor_scalar(nmax[:, i:i + 1], rden[:, i:i + 1], -1.0, None, ALU.mult).then_inc(S("x5_max"), 1)
                    dve.wait_ge(S("x5_probs"), since("x5_probs") + i + 1)
                    link("dve", dve, dve.reciprocal(rden[:, 16 + i:17 + i], den[:, i:i + 1]))
                    dve.tensor_scalar(pr(i)[:, 0:MEM], pr(i)[:, 0:MEM], rden[:, 16 + i:17 + i], None,
                                      ALU.mult).then_inc(S("x5_norm"), 1)
                j = i - 1
                if j >= 0:
                    h, t = j // T, j % T
                    dve.wait_ge(S("x5_turned"), since("x5_turned") + j + 1)
                    if t == 0 and h >= 1:
                        dve.wait_ge(S("x5_pv"), since("x5_pv") + 2 * h)
                    dve.tensor_copy(pxT[:, :, t * P:t * P + P],
                                    ps[:, 2 + j % 2, 0:MEM].rearrange("p (m q) -> p m q", m=MT)).then_inc(S("x5_pT"), 1)
            end_stage("dve", dve)
            residual_dve("r5")
            end_stage("dve", dve)

        def xattn_pool(pool):
            norm_pool("n5", T)
            for _ in range(4):
                end_stage("pool", pool)

        A6 = Area()
        wr = A6.take(KD, NG + NE)
        E12 = A6.take(T, 2, NE)
        both = A6.take(T, NE)
        lg = A6.take(T, NG + NE)
        tmp_e = A6.take(T, NE)
        tmp_f = A6.take(T, NE)
        tg = A6.take(T, 8 * NG)
        cnt = A6.take(8, NE)
        Gb = A6.take(8, NTAB + 1)
        Bb = A6.take(8, NTAB)
        Ab = A6.take(8, SLOT)
        be_f = A6.take(NTAB, NE)
        dests = A6.take(8, 4)
        gates = sb("gates", [P, 8])
        dest_i = sb("dest_i", [P, 8], I32)
        rowtok = sb("rowtok", [SLOT, NTAB], I32)
        tokcol = sb("tokcol", [SLOT, 4], I32)
        blk_e = sb("blk_e", [1, NTAB + 2], I32)
        n_blk = sb("n_blk", [1, 4], I32)
        tri = sb("tri", [P, P])
        ones = sb("ones", [P, P])
        tokid = sb("tokid", [P, T])
        hmid = nc.dram_tensor("hmid", [SEQ, D], F32).ap()
        ymid = nc.dram_tensor("ymid", [NBLK * SLOT, D], F32).ap()

        def moe_route_pe(pe, m):
            norm_pe(f"n{m}", xn_tile, T)
            end_stage("pe", pe)
            pe.wait_ge(S(f"wr{m}_in"), since(f"wr{m}_in") + 32)
            for t in range(T):
                last = accumulate(ps[:, t, 0:NG + NE], [(hT[:, k, t * P:t * P + P], wr[:, k, :]) for k in range(KD)])
                last.then_inc(S(f"logits{m}"), 1)
            pe.wait_ge(S(f"onehot{m}"), since(f"onehot{m}") + 1)
            for t in range(T):
                last = accumulate(ps[:, 4, t * NE:t * NE + NE],
                                  [(ones[:, :], both[:, u, :]) for u in range(t)] + [(tri[:, :], both[:, t, :])])
            accumulate(ps[:, 5, 0:NE], [(ones[:, :], both[:, u, :]) for u in range(T)]).then_inc(S(f"ranks{m}"), 1)
            pe.wait_ge(S(f"slots{m}"), since(f"slots{m}") + 1)
            accumulate(ps[0:SLOT, 6, 0:NTAB], [(Ab[:, c, :], Bb[:, c, :]) for c in range(8)]).then_inc(S(f"table{m}"), 1)
            end_stage("pe", pe)

        def moe_route_act(act, m, gain):
            norm_act(f"n{m}", x_tile, D, T, hT_tile, gains(gain))
            act.wait_ge(S(f"n{m}_xn"), since(f"n{m}_xn") + T)
            act.dma_start(hmid.rearrange("(t p) n -> p t n", p=P), xn[:, :, :]).then_inc(S(f"hmid{m}"), 16)
            end_stage("act", act)
            act.wait_ge(S(f"gshift{m}"), since(f"gshift{m}") + 1)
            nc.scalar.activation(tg[:, :, 4:8], tg[:, :, 4:8], ACT.Exp).then_inc(S(f"gexp{m}"), 1)
            act.wait_ge(S(f"vshift{m}"), since(f"vshift{m}") + 1)
            nc.scalar.activation(tg[:, :, 16:17], tg[:, :, 16:17], ACT.Exp).then_inc(S(f"vexp{m}"), 1)
            act.wait_ge(S(f"hmid{m}"), since(f"hmid{m}") + 16)
            end_stage("act", act)

        def moe_route_dve(dve, m, gain, bias):
            def L(i):
                link("dve", dve, i)
            norm_dve(f"n{m}", x_tile, D, T, xn_tile, hT_tile, gains(gain))
            end_stage("dve", dve)
            dve.wait_ge(S(f"logits{m}"), since(f"logits{m}") + T)
            gl, el = lg[:, :, 0:NG], lg[:, :, NG:NG + NE]
            L(dve.tensor_tensor(lg[:, :, :], ps[:, 0:T, 0:NG + NE], row(bias).unsqueeze(1).to_broadcast([P, T, NG + NE]),
                                ALU.add))
            b3 = lambda v, n: v.to_broadcast([P, T, n])
            r3 = lambda nm, n: row(nm).unsqueeze(1).to_broadcast([P, T, n])
            L(dve.tensor_reduce(tg[:, :, 0:1], gl, AX, ALU.max))
            dve.tensor_tensor(tg[:, :, 4:8], gl, b3(tg[:, :, 0:1], NG), ALU.subtract).then_inc(S(f"gshift{m}"), 1)
            L(dve.tensor_tensor(tg[:, :, 8:12], gl, b3(tg[:, :, 0:1], NG), ALU.is_equal))
            L(dve.tensor_tensor(tg[:, :, 8:12], tg[:, :, 8:12], r3("down_g", NG), ALU.mult))
            L(dve.tensor_reduce(tg[:, :, 1:2], tg[:, :, 8:12], AX, ALU.max))
            L(dve.tensor_tensor(tg[:, :, 8:12], r3("down_g", NG), b3(tg[:, :, 1:2], NG), ALU.is_equal))
            dve.wait_ge(S(f"gexp{m}"), since(f"gexp{m}") + 1)
            L(dve.tensor_reduce(tg[:, :, 2:3], tg[:, :, 4:8], AX, ALU.add))
            L(dve.tensor_scalar(tg[:, :, 12:16], tg[:, :, 8:12], -1.0, BIG, ALU.add, ALU.mult))
            for g in range(NG):
                L(dve.tensor_tensor(tmp_e[:, :, g * EG:g * EG + EG], el[:, :, g * EG:g * EG + EG],
                                    b3(tg[:, :, 12 + g:13 + g], EG), ALU.add))
            for c in range(2):
                v = tg[:, :, 18 + c:19 + c]
                one = E12[:, :, c, :]
                L(dve.tensor_reduce(v, tmp_e[:, :, :], AX, ALU.max))
                L(dve.tensor_tensor(one, tmp_e[:, :, :], b3(v, NE), ALU.is_equal))
                L(dve.tensor_tensor(one, one, r3("down_e", NE), ALU.mult))
                L(dve.tensor_reduce(tg[:, :, 20:21], one, AX, ALU.max))
                L(dve.tensor_tensor(one, r3("down_e", NE), b3(tg[:, :, 20:21], NE), ALU.is_equal))
                if c == 0:
                    L(dve.tensor_scalar(tmp_f[:, :, :], one, -3.0 * BIG, None, ALU.mult))
                    L(dve.tensor_tensor(tmp_e[:, :, :], tmp_e[:, :, :], tmp_f[:, :, :], ALU.add))
            L(dve.tensor_tensor(tg[:, :, 16:17], tg[:, :, 19:20], tg[:, :, 18:19], ALU.subtract))
            dve.tensor_tensor(both[:, :, :], E12[:, :, 0, :], E12[:, :, 1, :], ALU.add).then_inc(S(f"onehot{m}"), 1)
            dve.sem_inc(S(f"vshift{m}"), 1)
            dve.wait_ge(S(f"vexp{m}"), since(f"vexp{m}") + 1)
            L(dve.tensor_scalar(tg[:, :, 17:18], tg[:, :, 16:17], 1.0, None, ALU.add))
            L(dve.tensor_tensor(tg[:, :, 17:18], tg[:, :, 17:18], tg[:, :, 2:3], ALU.mult))
            gv = gates[:, :].rearrange("p (t c) -> p t c", c=2)
            L(dve.reciprocal(gv[:, :, 0:1], tg[:, :, 17:18]))
            L(dve.tensor_tensor(gv[:, :, 1:2], gv[:, :, 0:1], tg[:, :, 16:17], ALU.mult))
            dve.wait_ge(S(f"ranks{m}"), since(f"ranks{m}") + 1)
            L(dve.tensor_copy(cnt[:, 0, :], ps[:, 5, 0:NE]))
            L(dve.memset(cnt[:, 1, :], 0.0))
            L(dve.memset(cnt[:, 4, :], 1.0))
            for b in range(SEQ // SLOT):
                L(dve.scalar_tensor_tensor(cnt[:, 1, :], cnt[:, 0, :], float(b * SLOT), cnt[:, 1, :], ALU.is_gt, ALU.add))
            L(dve.tensor_tensor_scan(cnt[:, 2, :], cnt[:, 4, :], cnt[:, 1, :], 0.0, ALU.mult, ALU.add))
            L(dve.tensor_tensor(cnt[:, 3, :], cnt[:, 2, :], cnt[:, 1, :], ALU.subtract))
            L(dve.tensor_scalar(cnt[:, 3, :], cnt[:, 3, :], float(SLOT), None, ALU.mult))
            L(dve.tensor_tensor(tmp_e[:, :, :], ps[:, 4, 0:T * NE].rearrange("p (t e) -> p t e", t=T),
                                cnt[:, 3, :].unsqueeze(1).to_broadcast([P, T, NE]), ALU.add))
            dv = dests[:, :, 0].rearrange("p (t c) -> p t c", c=2)
            for c in range(2):
                L(dve.tensor_tensor(tmp_f[:, :, :], tmp_e[:, :, :], E12[:, :, c, :], ALU.mult))
                L(dve.tensor_reduce(dv[:, :, c:c + 1], tmp_f[:, :, :], AX, ALU.add))
            L(dve.tensor_copy(dest_i[:, :], dests[:, :, 0]))
            sh = lambda n: [P, 8, n]
            L(dve.tensor_tensor(Gb[:, :, :], dests[:, :, 0:1].to_broadcast(sh(NTAB + 1)),
                                row("iota_blk").unsqueeze(1).to_broadcast(sh(NTAB + 1)), ALU.is_ge))
            L(dve.tensor_tensor(Bb[:, :, :], Gb[:, :, 0:NTAB], Gb[:, :, 1:NTAB + 1], ALU.subtract))
            L(dve.tensor_reduce(dests[:, :, 1:2], Gb[:, :, 1:NTAB + 1], AX, ALU.add))
            L(dve.scalar_tensor_tensor(dests[:, :, 2], dests[:, :, 1], -float(SLOT), dests[:, :, 0], ALU.mult, ALU.add))
            L(dve.tensor_tensor(Ab[:, :, :], dests[:, :, 2:3].to_broadcast(sh(SLOT)),
                                row("iota_slot").unsqueeze(1).to_broadcast(sh(SLOT)), ALU.is_equal))
            for t in range(T):
                ins = dve.tensor_scalar(Bb[:, 2 * t:2 * t + 2, :], Bb[:, 2 * t:2 * t + 2, :], tokid[:, t:t + 1], None, ALU.mult)
                L(ins)
            dve.drain().then_inc(S(f"slots{m}"), 1)
            bshape = [1, NTAB, NE]
            L(dve.tensor_scalar(Gb[0:1, 0, 0:NTAB], row("iota_blk")[0:1, 0:NTAB], 1.0 / SLOT, None, ALU.mult))
            L(dve.tensor_tensor(be_f[0:1, :, :], Gb[0:1, 0, 0:NTAB].unsqueeze(2).to_broadcast(bshape),
                                cnt[0:1, 2, :].unsqueeze(1).to_broadcast(bshape), ALU.is_ge))
            L(dve.tensor_reduce(Gb[0:1, 1, 0:NTAB].unsqueeze(2), be_f[0:1, :, :], AX, ALU.add))
            L(dve.tensor_scalar(Gb[0:1, 1, 0:NTAB], Gb[0:1, 1, 0:NTAB], float(NE - 1), None, ALU.min))
            L(dve.tensor_copy(blk_e[0:1, 0:NTAB], Gb[0:1, 1, 0:NTAB]))
            L(dve.tensor_copy(n_blk[0:1, 0:1], cnt[0:1, 2, NE - 1:NE]))
            for c in range(2):
                turn = Gb[0:1, 3 + c, 0:NBLK // 4]
                L(dve.tensor_scalar(turn, Gb[0:1, 0, 2 * c:NBLK:4], cnt[0:1, 2, NE - 1:NE], None, ALU.is_lt))
                L(dve.tensor_reduce(Gb[0:1, 2, c:c + 1], turn, AX, ALU.add))
            L(dve.tensor_copy(n_blk[0:1, 1:3], Gb[0:1, 2, 0:2]))
            dve.wait_ge(S(f"table{m}"), since(f"table{m}") + 1)
            L(dve.tensor_copy(rowtok[:, :], ps[0:SLOT, 6, 0:NTAB]))
            end_stage("dve", dve)

        def moe_route_pool(pool, m, wg, wre):
            pool.dma_start(wr[:, :, 0:NG], wg.rearrange("(k p) n -> p k n", p=P)).then_inc(S(f"wr{m}_in"), 16)
            pool.dma_start(wr[:, :, NG:NG + NE], wre.rearrange("(k p) n -> p k n", p=P)).then_inc(S(f"wr{m}_in"), 16)
            norm_pool(f"n{m}", T)
            end_stage("pool", pool)
            end_stage("pool", pool)

        xg = work[:, 0:4 * D].rearrange("p (a n) -> p a n", a=4)
        yb = work[:, 4 * D:6 * D].rearrange("p (a n) -> p a n", a=4)
        xTb = work[:, 6 * D:7 * D].rearrange("p (a k s) -> p a k s", a=2, k=KD)
        hb = work[:, 7 * D:8 * D].rearrange("p (a n) -> p a n", a=2)
        gb = work[:, 8 * D:9 * D].rearrange("p (a n) -> p a n", a=2)
        hTb = work[:, 9 * D:10 * D].rearrange("p (a k s) -> p a k s", a=2, k=8)

        def step(eng):
            eng.sem_inc(S("steps"), 1)

        def expert_views(ff, places, g):
            size = EXPERT_RING * KD * 512 // places
            wv = ring[:, :, :].rearrange("p a n -> p (a n)")[:, g * size:(g + 1) * size]
            return (wv[:, 0:KD * ff].rearrange("p (k n) -> p k n", k=KD),
                    wv[:, KD * ff:2 * KD * ff].rearrange("p (k n) -> p k n", k=KD),
                    wv[:, 2 * KD * ff:2 * KD * ff + ff // P * D].rearrange("p (k n) -> p k n", n=D))

        def moe_pe(pe, m, ff, places):
            hw = ff // 2
            nch = hw // P
            nb = pe.value_load(n_blk[0:1, 0:1], min_val=0, max_val=NBLK)

            def turn_x(landed, q):
                pe.wait_ge(S(f"xg{m}_{q}"), landed)
                step(pe)
                for k in range(KD):
                    last = nc.tensor.transpose(ps[:, 4, k * SLOT:k * SLOT + SLOT], xg[0:SLOT, q, k * P:k * P + P],
                                               ident[0:SLOT, 0:SLOT])
                last.then_inc(S(f"xT{m}_turned"), 1)

            for g in range(places):
                pe.sem_inc(S(f"y{m}_sum{g}"), 1)
            pe.sem_inc(S(f"h{m}_sum"), 2 * places)
            turn_x(16, 0)
            with pe.Fori(0, NBLK // 4) as i:
                for q in range(4):
                    b, p, g = i * 4 + q, q % 2, q % places
                    use = i * (4 // places) + q // places
                    if p == 0:
                        pair = pe.If(b < nb)
                        pair.__enter__()
                    w1, w3, w2 = expert_views(ff, places, g)
                    pe.wait_ge(S(f"up{m}_{g}"), use * 32 + 32)
                    pe.wait_ge(S(f"xT{m}_ready"), b + 1)
                    pe.wait_ge(S(f"h{m}_ready"), b + 1)
                    for w, bank in ((w1, 0), (w3, 1)):
                        for k in range(KD):
                            for hf in range(2):
                                last = nc.tensor.matmul(ps[64 * hf:64 * hf + 64, bank, 0:hw], xTb[:, p, k, :],
                                                        w[:, k, hf * hw:hf * hw + hw],
                                                        start=k == 0, stop=k == KD - 1)
                        last.then_inc(S(f"h{m}_sum"), 1)
                    turn_x(i * 16 + (16 if q < 3 else 32), (q + 1) % 4)
                    pe.wait_ge(S(f"h{m}_ready"), b + 2)
                    pe.wait_ge(S(f"hT{m}_ready"), b + 1)
                    for c in range(nch):
                        last = nc.tensor.transpose(ps[:, 5, c * P:c * P + P], hb[:, p, c * P:c * P + P], ident[:, :])
                    last.then_inc(S(f"h{m}_turned"), 1)
                    pe.wait_ge(S(f"down{m}_{g}"), use * 16 + 16)
                    pe.wait_ge(S(f"hT{m}_ready"), b + 2)
                    pe.wait_ge(S(f"y{m}_ready"), b + 1)
                    for c in range(2 * nch):
                        for hf in range(2):
                            last = nc.tensor.matmul(ps[64 * hf:64 * hf + 64, 6, :],
                                                    hTb[:, p, (c % nch) * 2 + c // nch, :],
                                                    w2[:, c, hf * 512:hf * 512 + 512],
                                                    start=c == 0, stop=c == 2 * nch - 1)
                    last.then_inc(S(f"y{m}_sum{g}"), 1)
                    if p == 1:
                        pair.__exit__(None, None, None)
            end_stage("pe", pe)

        def moe_act(act, m, ff, places):
            hw = ff // 2
            nb = act.value_load(n_blk[0:1, 0:1], min_val=0, max_val=NBLK)
            act.sem_inc(S(f"y{m}_ready"), 1)
            for q in range(4):
                act.sem_inc(S(f"y{m}_store{q}"), 32)
            with act.Fori(0, NBLK // 4) as i:
                for q in range(4):
                    b, p, g = i * 4 + q, q % 2, q % places
                    use = i * (4 // places) + q // places
                    if p == 0:
                        pair = act.If(b < nb)
                        pair.__enter__()
                    act.wait_ge(S(f"h{m}_sum"), b * 2 + 2 * places + 1)
                    nc.scalar.activation(gb[:, p, 0:hw], ps[:, 0, 0:hw], ACT.Silu).then_inc(S(f"silu{m}"), 1)
                    act.wait_ge(S(f"y{m}_sum{g}"), use + 2)
                    act.wait_ge(S(f"y{m}_store{q}"), i * 32 + 32)
                    nc.scalar.copy(yb[:, q, :], ps[:, 6, :]).then_inc(S(f"y{m}_ready"), 1)
                    act.wait_ge(S(f"y{m}_ready"), b + 2)
                    for hf in range(2):
                        act.dma_start(ymid[bass.ds(b * SLOT, SLOT), hf * 512:hf * 512 + 512],
                                      yb[64 * hf:64 * hf + 64, q, :]).then_inc(S(f"y{m}_store{q}"), 16)
                    if p == 1:
                        pair.__exit__(None, None, None)
            end_stage("act", act)

        def moe_dve(dve, m, ff, gain, places):
            hw = ff // 2
            nch = hw // P
            nb = dve.value_load(n_blk[0:1, 0:1], min_val=0, max_val=NBLK)

            def take_x(n, p):
                dve.wait_ge(S(f"xT{m}_turned"), n + 1)
                g0 = COLS[gain][0]
                dve.tensor_tensor(xTb[:, p, :, :], ps[:, 4, :].rearrange("p (k s) -> p k s", k=KD),
                                  cols[:, g0:g0 + KD].unsqueeze(2).to_broadcast([P, KD, SLOT]), ALU.mult
                                  ).then_inc(S(f"xT{m}_ready"), 1)

            dve.sem_inc(S(f"h{m}_ready"), 1)
            dve.sem_inc(S(f"hT{m}_ready"), 1)
            take_x(0, 0)
            with dve.Fori(0, NBLK // 4) as i:
                for q in range(4):
                    b, p = i * 4 + q, q % 2
                    if p == 0:
                        pair = dve.If(b < nb)
                        pair.__enter__()
                    dve.wait_ge(S(f"silu{m}"), b + 1)
                    dve.wait_ge(S(f"h{m}_sum"), b * 2 + 2 * places + 2)
                    dve.tensor_tensor(hb[:, p, 0:hw], gb[:, p, 0:hw], ps[:, 1, 0:hw], ALU.mult).then_inc(
                        S(f"h{m}_ready"), 1)
                    take_x(b + 1, 1 - p)
                    dve.wait_ge(S(f"h{m}_turned"), b + 1)
                    dve.tensor_copy(hTb[:, p, 0:2 * nch, :],
                                    ps[:, 5, 0:nch * P].rearrange("p (c s) -> p c s", s=SLOT)).then_inc(
                        S(f"hT{m}_ready"), 1)
                    if p == 1:
                        pair.__exit__(None, None, None)
            end_stage("dve", dve)

        def moe_pool(pool, m):
            pool.wait_ge(S("ymid_zeroed"), 16)
            nb = pool.value_load(n_blk[0:1, 0:1], min_val=0, max_val=NBLK)
            turns = [pool.value_load(n_blk[0:1, 1 + c:2 + c], min_val=4, max_val=NBLK // 4) for c in range(2)]

            def gather(b, q, n):
                nc.gpsimd.tensor_copy(tokcol[:, q:q + 1], rowtok[:, bass.ds(b, 1)]).then_inc(S(f"tokcol{m}"), 1)
                pool.wait_ge(S(f"tokcol{m}"), n + 1)
                step(pool)
                pool.indirect_dma_start(out=xg[0:SLOT, q, :], out_offset=None, in_=hmid,
                                        in_offset=bass.IndirectOffsetOnAxis(ap=tokcol[:, q:q + 1], axis=0)
                                        ).then_inc(S(f"xg{m}_{q}"), 16)

            for q in range(4):
                gather(q, q, q)
            with pool.Fori(0, NBLK // 4) as i:
                for q in range(4):
                    b, p = i * 4 + q, q % 2
                    if p == 0:
                        pair = pool.If(b < nb)
                        pair.__enter__()
                    pool.wait_ge(S(f"xg{m}_{q}"), i * 16 + 16)
                    pool.wait_ge(S(f"xT{m}_turned"), b + 1)
                    gather(b + 4, q, b + 4)
                    if p == 1:
                        pair.__exit__(None, None, None)
            for q in range(4):
                pool.wait_ge(S(f"y{m}_store{q}"), turns[q // 2] * 32 + 32)
                pool.wait_ge(S(f"xg{m}_{q}"), turns[q // 2] * 16 + 16)
            step(pool)
            end_stage("pool", pool)

        def moe_sp(sp, m, wa, wb, wc, ff, places):
            nb = sp.value_load(n_blk[0:1, 0:1], min_val=0, max_val=NBLK)
            with sp.Fori(0, NBLK // 4) as i:
                for q in range(4):
                    b, p, g = i * 4 + q, q % 2, q % places
                    use = i * (4 // places) + q // places
                    if p == 0:
                        pair = sp.If(b < nb)
                        pair.__enter__()
                    e = sp.value_load(blk_e[0:1, bass.ds(b, 1)], min_val=0, max_val=NE - 1)
                    views = expert_views(ff, places, g)
                    sp.wait_ge(S(f"h{m}_sum"), b * 2 + 2)
                    for w, dst in ((wa, views[0]), (wb, views[1])):
                        sp.dma_start(dst, w[0, bass.ds(e, 1)].rearrange("o (k p) n -> p (o k) n", p=P)
                                     ).then_inc(S(f"up{m}_{g}"), 16)
                    sp.wait_ge(S(f"y{m}_sum{g}"), use + 1)
                    sp.dma_start(views[2], wc[0, bass.ds(e, 1)].rearrange("o (k p) n -> p (o k) n", p=P)
                                 ).then_inc(S(f"down{m}_{g}"), 16)
                    if p == 1:
                        pair.__exit__(None, None, None)

        yg = lambda j: work[:, (j % 4) * D:(j % 4) * D + D]

        def combine_pool(pool, m):
            for j in range(8):
                if j >= 4:
                    pool.wait_ge(S(f"comb{m}"), since(f"comb{m}") + j - 3)
                pool.indirect_dma_start(out=yg(j), out_offset=None, in_=ymid,
                                        in_offset=bass.IndirectOffsetOnAxis(ap=dest_i[:, j:j + 1], axis=0)
                                        ).then_inc(S(f"yg{m}_{j % 4}"), 16)
            end_stage("pool", pool)

        def combine_dve(dve, m):
            for j in range(8):
                t = j // 2
                dve.wait_ge(S(f"yg{m}_{j % 4}"), since(f"yg{m}_{j % 4}") + 16 * (j // 4 + 1))
                dve.scalar_tensor_tensor(x[:, t, :], yg(j), gates[:, j:j + 1], x[:, t, :], ALU.mult,
                                         ALU.add).then_inc(S(f"comb{m}"), 1)
                dve.wait_ge(S(f"comb{m}"), since(f"comb{m}") + j + 1)
            end_stage("dve", dve)

        STAGES_TO_MOE1 = 2 + 1 + 1 + 1 + 2 + 4 + 2

        sp_ = lambda at, *shape: (lambda v: v if len(shape) == 1 else v.rearrange("p (a b) -> p a b", a=shape[0]))(
            spare[:, at:at + int(np.prod(shape))])
        wk_ = lambda at, *shape: (lambda v: v if len(shape) == 1 else v.rearrange("p (a b) -> p a b", a=shape[0]))(
            work[:, at:at + int(np.prod(shape))])
        xn_flat = xn[:, :, :].rearrange("p t n -> p (t n)")
        xf_ = lambda at, *shape: (lambda v: v if len(shape) == 1 else v.rearrange("p (a b) -> p a b", a=shape[0]))(
            xn_flat[:, at:at + int(np.prod(shape))])
        final_g = hT[:, 0:2, :].rearrange("p k n -> p (k n)")
        uT = sp_(1024, NU, SEQ)
        ysT = sp_(3072, NU, SEQ)
        fbuf = spare[:, 5248:5248 + 3 * SEQ].rearrange("p (a n) -> p a n", a=3)
        wf = sb("wf", [P, KD * H2])
        wfv = wf[:, :].rearrange("p (k n) -> p k n", k=KD)
        tabC = wk_(0, SS, CH)
        tabS = wk_(2048, SS, CH)
        Zr, Zi = wk_(4096, 4, SEQ), wk_(6144, 4, SEQ)
        prod = [[wk_(8192, 4, SEQ)[:, i, :] for i in range(4)],
                [junk[:, 0:512], junk[:, 512:1024], junk2[:, 0:512], junk2[:, 512:1024]]]
        BT = wk_(10240, 8, P)
        CT = wk_(11264, 8, P)
        BP, CP = xf_(0, 8, P), xf_(1024, 8, P)
        Cn = xf_(2048, 2, 64)
        Braw = xf_(2176, 2, SS * 16)
        Bbar = xf_(2688, 2, SS * 16)
        sc = xf_(3200, 20, SS)
        carry = xf_(3520, 8, 4)

        def final_act(act):
            for t in range(T):
                nc.scalar.activation(junk[:, :], x_tile(t), ACT.Square, accum_out=st[:, t:t + 1]).then_inc(S("nf_sumsq"), 1)
                act.wait_ge(S("nf_sumsq"), since("nf_sumsq") + t + 1)
            end_stage("act", act)
            norm_act("n7", x_tile, D, T, hT_tile, gains("mix2_g"))
            end_stage("act", act)

        def final_dve(dve):
            dve.wait_ge(S("nf_sumsq"), since("nf_sumsq") + T)
            dve.tensor_scalar(st[:, 8:12], st[:, 0:4], 1.0 / D, EPS, ALU.mult, ALU.add).then_inc(S("nf_var"), 1)
            dve.wait_ge(S("nf_rstd"), since("nf_rstd") + 1)
            dve.wait_ge(S("fg_in"), 16)
            for t in range(T):
                dve.scalar_tensor_tensor(x_tile(t), x_tile(t), st[:, 16 + t:17 + t], final_g, ALU.mult, ALU.mult)
            end_stage("dve", dve)
            norm_dve("n7", x_tile, D, T, xn_tile, hT_tile, gains("mix2_g"))
            end_stage("dve", dve)

        def s5_load_pool(pool):
            for i, nm in enumerate(("ssm_B_re_2", "ssm_B_im_2")):
                pool.dma_start(Braw[:, i, :].rearrange("p (s c) -> p s c", s=SS),
                               a[nm][0].rearrange("g p c -> (g p) c").rearrange("(s p) c -> p s c", p=P)
                               ).then_inc(S("B_in"), 16)
            pool.dma_start(wfv, a["w_in_2"][0][:, 1536:1544].rearrange("(k p) n -> p k n", p=P)).then_inc(S("wf_in"), 16)

        def s5_prep_pe(pe):
            arrived(pe, "u")
            for f in range(NU):
                accumulate(ps[:, f, :], [(weight("u")[:, k, f * P:f * P + P], hT[:, k, :]) for k in range(KD)]
                           ).then_inc(S("u_sum"), 1)
            pe.wait_ge(S("u_sum"), since("u_sum") + NU)
            pe.sem_inc(S("w_used1"), 1)
            pe.wait_ge(S("wf_in"), 16)
            accumulate(ps[0:H2, 4, :], [(wfv[:, k, :], hT[:, k, :]) for k in range(KD)]).then_inc(S("f_sum"), 1)
            end_stage("pe", pe)

        def s5_prep_act(act):
            nc.scalar.activation(sc[:, 0, :], col("log_dt", 0, SS), ACT.Exp).then_inc(S("sp_exp"), 1)
            act.wait_ge(S("sp_ra"), 1)
            nc.scalar.activation(sc[:, 3, :], sc[:, 1, :], ACT.Exp).then_inc(S("sp_exp"), 1)
            for f in range(NU):
                act.wait_ge(S("u_sum"), since("u_sum") + f + 1)
                nc.scalar.copy(uT[:, f, :], ps[:, f, :])
            act.wait_ge(S("f_sum"), 1)
            nc.scalar.copy(fbuf[0:H2, 0, :], ps[0:H2, 4, :])
            act.wait_ge(S("sp_ang"), 1)
            nc.scalar.activation(sc[:, 5:7, :], sc[:, 5:7, :], ACT.Sin).then_inc(S("sp_sin"), 1)
            act.wait_ge(S("sp_tab"), 1)
            nc.scalar.activation(tabC, tabC, ACT.Sin)
            nc.scalar.activation(tabS, tabS, ACT.Sin)
            end_stage("act", act)

        def s5_prep_dve(dve):
            def L(i):
                link("dve", dve, i)
            L(dve.memset(BP, 0.0))
            ar, ai = col("a_re", 0, SS), col("a_im", 0, SS)
            dve.wait_ge(S("sp_exp"), 1)
            L(dve.tensor_tensor(sc[:, 1, :], ar, sc[:, 0, :], ALU.mult))
            dve.sem_inc(S("sp_ra"), 1)
            L(dve.tensor_tensor(sc[:, 2, :], ai, sc[:, 0, :], ALU.mult))
            sin_cos_dve(dve, sc[:, 2, :], sc[:, 4, :], sc[:, 5, :], sc[:, 6, :], True)
            dve.sem_inc(S("sp_ang"), 1)
            L(dve.tensor_scalar(sc[:, 7, :], sc[:, 2, :], 3072.0, None, ALU.add))
            L(dve.tensor_scalar(sc[:, 7, :], sc[:, 7, :], -3072.0, None, ALU.add))
            L(dve.tensor_tensor(sc[:, 8, :], sc[:, 2, :], sc[:, 7, :], ALU.subtract))
            full = [P, SS, CH]
            steps = row("iota_chunk").unsqueeze(1).to_broadcast(full)
            L(dve.tensor_tensor(tabS, sc[:, 7, :].unsqueeze(2).to_broadcast(full), steps, ALU.mult))
            turn = wk_(4096, SS, CH)
            fl = lambda v: v.rearrange("p a b -> p (a b)")
            L(dve.tensor_scalar(fl(turn), fl(tabS), 1.0 / TWO_PI, ROUND, ALU.mult, ALU.add))
            L(dve.tensor_scalar(fl(turn), fl(turn), -ROUND, None, ALU.add))
            for c in split_two_pi():
                L(dve.scalar_tensor_tensor(fl(tabS), fl(turn), -c, fl(tabS), ALU.mult, ALU.add))
            L(dve.tensor_tensor(turn, sc[:, 8, :].unsqueeze(2).to_broadcast(full), steps, ALU.mult))
            L(dve.tensor_tensor(tabS, tabS, turn, ALU.add))
            L(dve.tensor_scalar(fl(turn), fl(tabS), math.pi / 2, -TWO_PI, ALU.is_gt, ALU.mult))
            L(dve.scalar_tensor_tensor(fl(tabC), fl(tabS), math.pi / 2, fl(turn), ALU.add, ALU.add))
            L(dve.tensor_scalar(fl(tabC), fl(tabC), -math.pi, math.pi, ALU.max, ALU.min))
            L(dve.tensor_scalar(fl(tabS), fl(tabS), -math.pi, math.pi, ALU.max, ALU.min))
            dve.sem_inc(S("sp_tab"), 1)
            dve.wait_ge(S("sp_exp"), 2)
            dve.wait_ge(S("sp_sin"), 1)
            v = lambda i: sc[:, i, :]
            L(dve.tensor_tensor(v(9), v(3), v(5), ALU.mult))
            L(dve.tensor_scalar(v(9), v(9), -1.0, None, ALU.add))
            L(dve.tensor_tensor(v(10), v(3), v(6), ALU.mult))
            L(dve.tensor_tensor(v(11), ar, ar, ALU.mult))
            L(dve.tensor_tensor(v(12), ai, ai, ALU.mult))
            L(dve.tensor_tensor(v(11), v(11), v(12), ALU.add))
            L(dve.reciprocal(v(11), v(11)))
            L(dve.tensor_tensor(v(12), v(9), ar, ALU.mult))
            L(dve.tensor_tensor(v(13), v(10), ai, ALU.mult))
            L(dve.tensor_tensor(v(12), v(12), v(13), ALU.add))
            L(dve.tensor_tensor(v(12), v(12), v(11), ALU.mult))
            L(dve.tensor_tensor(v(13), v(10), ar, ALU.mult))
            L(dve.tensor_tensor(v(14), v(9), ai, ALU.mult))
            L(dve.tensor_tensor(v(13), v(13), v(14), ALU.subtract))
            L(dve.tensor_tensor(v(13), v(13), v(11), ALU.mult))
            dve.wait_ge(S("B_in"), 32)
            b16 = [P, SS, 16]
            br = Braw[:, 0, :].rearrange("p (s c) -> p s c", s=SS)
            bi = Braw[:, 1, :].rearrange("p (s c) -> p s c", s=SS)
            o = [Bbar[:, i, :].rearrange("p (s c) -> p s c", s=SS) for i in range(2)]
            tq = wk_(6144, SS, 16)
            kr, ki = (v(i).unsqueeze(2).to_broadcast(b16) for i in (12, 13))
            L(dve.tensor_tensor(o[0], br, kr, ALU.mult))
            L(dve.tensor_tensor(tq, bi, ki, ALU.mult))
            L(dve.tensor_tensor(o[0], o[0], tq, ALU.subtract))
            L(dve.tensor_tensor(o[1], bi, kr, ALU.mult))
            L(dve.tensor_tensor(tq, br, ki, ALU.mult))
            L(dve.tensor_tensor(o[1], o[1], tq, ALU.add))
            end_stage("dve", dve)

        def s5_pe(pe):
            for q in range(NU):
                pe.wait_ge(S("s5_padded"), q + 1)
                if q:
                    pe.wait_ge(S("s5_yout"), q)
                for i in range(8):
                    nc.tensor.transpose(ps[:, i // 4, (i % 4) * P:(i % 4) * P + P], BP[:, i, :], ident[:, :])
                for i in range(8):
                    last = nc.tensor.transpose(ps[:, 2 + i // 4, (i % 4) * P:(i % 4) * P + P], CP[:, i, :], ident[:, :])
                last.then_inc(S("s5_turned"), 1)
                pe.wait_ge(S("s5_mats"), q + 1)
                for j in range(4):
                    n = 4 * q + j
                    if n >= 2:
                        pe.wait_ge(S("s5_in_read"), n - 1)
                    for c in range(2):
                        last = nc.tensor.matmul(ps[:, 4 + 2 * (j % 2) + c, :], BT[:, 4 * c + j, :], uT[:, q, :],
                                                start=True, stop=True)
                    last.then_inc(S("s5_in"), 1)
                for j in range(4):
                    pe.wait_ge(S("s5_state"), 2 * (4 * q + j + 1))
                    for c in range(2):
                        last = nc.tensor.matmul(ps[:, 0, :], CT[:, 4 * c + j, :], (Zr, Zi)[c][:, j, :],
                                                start=j == 0 and c == 0, stop=j == 3 and c == 1)
                last.then_inc(S("s5_y"), 1)
            end_stage("pe", pe)

        def s5_act(act):
            for q in range(NU):
                for i, nm in enumerate(("ssm_C_re_2", "ssm_C_im_2")):
                    act.dma_start(Cn[:, i, :], a[nm][0].rearrange("g c p -> (g c) p")[q * P:q * P + P, :]).then_inc(
                        S("C_in"), 16)
                if q:
                    act.wait_ge(S("s5_turned"), q)
                act.wait_ge(S("C_in"), 32 * (q + 1))
                nc.scalar.mul(Cn[:, 1, :], Cn[:, 1, :], -1.0).then_inc(S("C_neg"), 1)
                act.wait_ge(S("C_neg"), q + 1)
                for c in range(2):
                    for j in range(4):
                        for h in range(2):
                            g = 2 * j + h
                            nc.scalar.activation(BP[:, 4 * c + j, g * 16:g * 16 + 16],
                                                 Bbar[:, c, (4 * q + j) * 16:(4 * q + j) * 16 + 16], ACT.Identity,
                                                 scale=col("half", h)).then_inc(S("s5_pad_steps"), 1)
                            nc.scalar.activation(CP[:, 4 * c + j, h * 64:h * 64 + 64], Cn[:, c, :], ACT.Identity,
                                                 scale=col("group_of", g)).then_inc(S("s5_pad_steps"), 1)
                act.wait_ge(S("s5_pad_steps"), 32 * (q + 1))
                act.sem_inc(S("s5_padded"), 1)
                act.wait_ge(S("s5_turned"), q + 1)
                if q:
                    act.wait_ge(S("s5_y"), q)
                for h in range(2):
                    nc.scalar.copy(BT[:, 4 * h:4 * h + 4, :], ps[:, h, :].rearrange("p (a b) -> p a b", a=4)).then_inc(
                        S("s5_mat_steps"), 1)
                    nc.scalar.copy(CT[:, 4 * h:4 * h + 4, :], ps[:, 2 + h, :].rearrange("p (a b) -> p a b", a=4)
                                   ).then_inc(S("s5_mat_steps"), 1)
                act.wait_ge(S("s5_mat_steps"), 4 * (q + 1))
                act.sem_inc(S("s5_mats"), 1)
            end_stage("act", act)

        def s5_dve(dve):
            def L(i):
                link("dve", dve, i)
            v4 = lambda v: v.rearrange("p (c t) -> p c t", t=CH)
            k = 0
            for q in range(NU):
                if q:
                    dve.wait_ge(S("s5_y"), q)
                for j in range(4):
                    s = 4 * q + j
                    C = tabC[:, s, :].unsqueeze(1).to_broadcast([P, T, CH])
                    Sn = tabS[:, s, :].unsqueeze(1).to_broadcast([P, T, CH])
                    re, im = (v4(ps[:, 4 + 2 * (j % 2) + c, :]) for c in range(2))
                    dve.wait_ge(S("s5_in"), s + 1)
                    if k >= 2:
                        dve.wait_ge(S("s5_added"), 2 * (k - 1))
                    pb = prod[k % 2]
                    for o, (l, r) in enumerate(((re, C), (im, Sn), (im, C), (re, Sn))):
                        ins = dve.tensor_tensor(v4(pb[o]), l, r, ALU.mult).then_inc(S("s5_prod"), 1)
                    dve.wait_ge(S("s5_prod"), 4 * (k + 1))
                    dve.sem_inc(S("s5_in_read"), 1)
                    k += 1
                dve.wait_ge(S("s5_added"), 2 * k)
                for c in range(T):
                    for j in range(4):
                        s = 4 * q + j
                        r = sc[:, 3, s:s + 1].to_broadcast([P, CH])
                        for z, Z in enumerate((Zr, Zi)):
                            zc = Z[:, j, c * CH:c * CH + CH]
                            ini = 0.0 if c == 0 else carry[:, z, j:j + 1]
                            dve.tensor_tensor_scan(zc, r, zc, ini, ALU.mult, ALU.add).then_inc(S("s5_scan"), 1)
                    dve.wait_ge(S("s5_scan"), 8 * (4 * q + c + 1))
                    if c < T - 1:
                        e = c * CH + CH - 1
                        C = tabC[:, 4 * q:4 * q + 4, CH - 1]
                        Sn = tabS[:, 4 * q:4 * q + 4, CH - 1]
                        L(dve.tensor_tensor(carry[:, 2, :], Zr[:, :, e], C, ALU.mult))
                        L(dve.tensor_tensor(carry[:, 3, :], Zi[:, :, e], Sn, ALU.mult))
                        L(dve.tensor_tensor(carry[:, 4, :], Zr[:, :, e], Sn, ALU.mult))
                        L(dve.tensor_tensor(carry[:, 5, :], Zi[:, :, e], C, ALU.mult))
                        L(dve.tensor_tensor(carry[:, 0, :], carry[:, 2, :], carry[:, 3, :], ALU.subtract))
                        L(dve.tensor_tensor(carry[:, 1, :], carry[:, 4, :], carry[:, 5, :], ALU.add))
                for j in range(4):
                    s = 4 * q + j
                    C = tabC[:, s, :].unsqueeze(1).to_broadcast([P, T, CH])
                    Sn = tabS[:, s, :].unsqueeze(1).to_broadcast([P, T, CH])
                    dve.wait_ge(S("s5_added"), 2 * (k - 1))
                    pb = prod[k % 2]
                    zr, zi = v4(Zr[:, j, :]), v4(Zi[:, j, :])
                    for o, (l, r) in enumerate(((zr, C), (zi, Sn), (zr, Sn), (zi, C))):
                        dve.tensor_tensor(v4(pb[o]), l, r, ALU.mult).then_inc(S("s5_prod"), 1)
                    dve.wait_ge(S("s5_prod"), 4 * (k + 1))
                    k += 1
                dve.wait_ge(S("s5_y"), q + 1)
                dve.scalar_tensor_tensor(ysT[:, q, :], uT[:, q, :], col("ssm_d", q), ps[:, 0, :], ALU.mult,
                                         ALU.add).then_inc(S("s5_yout"), 1)
            end_stage("dve", dve)

        def s5_pool(pool):
            k = 0
            for q in range(NU):
                for back in range(2):
                    for j in range(4):
                        pb = prod[k % 2]
                        pool.wait_ge(S("s5_prod"), 4 * (k + 1))
                        nc.gpsimd.tensor_tensor(Zr[:, j, :], pb[0], pb[1], ALU.subtract if back else ALU.add
                                                ).then_inc(S("s5_added"), 1)
                        nc.gpsimd.tensor_tensor(Zi[:, j, :], pb[2], pb[3], ALU.add if back else ALU.subtract
                                                ).then_inc(S("s5_added"), 1)
                        pool.wait_ge(S("s5_added"), 2 * (k + 1))
                        if back:
                            pool.sem_inc(S("s5_state"), 2)
                        k += 1
            end_stage("pool", pool)

        gl_a = wk_(4096, NU, SEQ)
        gl_t = wk_(6144, NU, SEQ)
        fl3 = lambda v: v.rearrange("p a b -> p (a b)")

        def glu_pe(pe):
            arrived(pe, "glu")
            pe.wait_ge(S("gelu"), 1)
            for f in range(NU):
                accumulate(ps[:, f, :], [(weight("glu")[:, k, f * P:f * P + P], gl_a[:, k, :]) for k in range(NU)]
                           ).then_inc(S("glu_sum"), 1)
            pe.wait_ge(S("glu_sum"), since("glu_sum") + NU)
            pe.sem_inc(S("w_used1"), 1)
            end_stage("pe", pe)

        def glu_act(act):
            act.wait_ge(S("gelu_in"), 1)
            nc.scalar.activation(fl3(gl_t), fl3(gl_t), ACT.Tanh, scale=math.sqrt(2 / math.pi)).then_inc(S("gelu_tanh"), 1)
            for f in range(NU):
                act.wait_ge(S("glu_sum"), since("glu_sum") + f + 1)
                if f == 0:
                    act.wait_ge(S("gelu"), 1)
                nc.scalar.activation(gl_t[:, f, :], ps[:, f, :], ACT.Sigmoid).then_inc(S("glu_sig"), 1)
            end_stage("act", act)

        def glu_dve(dve):
            def L(i):
                link("dve", dve, i)
            y, t_ = fl3(ysT), fl3(gl_t)
            L(dve.tensor_tensor(t_, y, y, ALU.mult))
            L(dve.tensor_scalar(t_, t_, 0.044715, 1.0, ALU.mult, ALU.add))
            dve.tensor_tensor(t_, t_, y, ALU.mult).then_inc(S("gelu_in"), 1)
            dve.wait_ge(S("gelu_tanh"), 1)
            L(dve.scalar_tensor_tensor(t_, t_, 1.0, y, ALU.add, ALU.mult))
            dve.tensor_scalar(fl3(gl_a), t_, 0.5, None, ALU.mult).then_inc(S("gelu"), 1)
            for f in range(NU):
                dve.wait_ge(S("glu_sig"), f + 1)
                dve.tensor_tensor(ysT[:, f, :], gl_a[:, f, :], gl_t[:, f, :], ALU.mult)
            end_stage("dve", dve)

        v2 = wk_(0, T, 512)
        qk = wk_(2048, 8, 512)
        q2 = wk_(6144, H2, SEQ)
        k2 = wk_(10240, 4, SEQ)
        Fb = xf_(0, H2, SEQ)
        o2 = wk_(2048, T, 512)
        oT = sp_(1024, 4, SEQ)
        causal = sp_(5120, P)
        pT2 = lambda i: spare[:, 7168 + (i % 2) * 512:7680 + (i % 2) * 512]
        qstat = sb("qstat", [P, 3 * 64])
        halves64 = sb("halves64", [P, 64])
        fmid = nc.dram_tensor("fmid", [H2, SEQ], F32).ap()

        def fox_in_pe(pe):
            for c, nm in enumerate(("q", "k", "v")):
                arrived(pe, nm)
                for t in range(T):
                    g = 4 * c + t
                    if g >= 8:
                        pe.wait_ge(S("fox_out"), since("fox_out") + g - 7)
                    accumulate(ps[:, g % 8, :], [(hT[:, k, t * P:t * P + P], weight(nm)[:, k, :]) for k in range(KD)]
                               ).then_inc(S("fox_sum"), 1)
                pe.wait_ge(S("fox_sum"), since("fox_sum") + 4 * (c + 1))
                pe.sem_inc(S("w_used1"), 1)
            end_stage("pe", pe)
            for i in range(8):
                for t in range(T):
                    last = nc.tensor.transpose(ps[:, i, t * P:t * P + P],
                                               qk[:, (i // 4) * T + t, (i % 4) * P:(i % 4) * P + P], ident[:, :])
                last.then_inc(S("fox_turned"), 1)
            end_stage("pe", pe)

        def fox_in_act(act):
            act.dma_start(causal, a["causal"]).then_inc(S("causal_in"), 16)
            act.wait_ge(S("lf_abs"), 1)
            nc.scalar.activation(fbuf[0:H2, 1, :], fbuf[0:H2, 1, :], ACT.Exp, scale=-1.0).then_inc(S("lf_exp"), 1)
            act.wait_ge(S("lf_exp"), 1)
            nc.scalar.activation(fbuf[0:H2, 1, :], fbuf[0:H2, 1, :], ACT.Ln, bias=1.0).then_inc(S("lf_ln"), 1)
            for g in range(12):
                act.wait_ge(S("fox_sum"), since("fox_sum") + g + 1)
                if g < 8:
                    if g >= 2:
                        act.wait_ge(S("fox_ss"), g - 1)
                    nc.scalar.activation(junk[:, (g % 2) * 512:(g % 2) * 512 + 512], ps[:, g, :], ACT.Square).then_inc(
                        S("fox_sq"), 1)
                    nc.scalar.copy(qk[:, g, :], ps[:, g, :]).then_inc(S("fox_out"), 1)
                else:
                    nc.scalar.copy(v2[:, g - 8, :], ps[:, g - 8, :]).then_inc(S("fox_out"), 1)
            act.wait_ge(S("F_done"), 1)
            act.dma_start(fmid, fbuf[0:H2, 2, :]).then_inc(S("F_mid"), 16)
            act.wait_ge(S("F_mid"), 16)
            act.dma_start(Fb, fmid.unsqueeze(0).to_broadcast([P, H2, SEQ])).then_inc(S("F_in"), 16)
            act.wait_ge(S("F_in"), 16)
            end_stage("act", act)
            for i in range(0, 8, 2):
                act.wait_ge(S("fox_turned"), i + 1)
                fox_place(act, i)
            end_stage("act", act)

        def fox_place(eng, i):
            for h in range(2):
                r = slice(64 * h, 64 * h + 64)
                dst = q2[r, 2 * i + h, :] if i < 4 else k2[r, i - 4, :]
                g = qn_scaled[r, 0:1] if i < 4 else col("kn_g", 0, 1)[r]
                if eng is nc.vector:
                    eng.tensor_scalar(dst, ps[r, i, :], g, None, ALU.mult)
                else:
                    nc.scalar.activation(dst, ps[r, i, :], ACT.Identity, scale=g)

        qn_scaled = sb("qn_scaled", [P, 1])

        def fox_in_dve(dve):
            def L(i):
                link("dve", dve, i)
            L(dve.memset(halves64[:, :], -0.5))
            L(dve.memset(q2, 0.0))
            L(dve.tensor_scalar(qn_scaled[:, :], col("qn_g"), 0.125, None, ALU.mult))
            f0, f1, f2 = (fbuf[0:H2, i, :] for i in range(3))
            L(dve.tensor_scalar(f0, f0, col("forget_b")[0:H2], None, ALU.add))
            L(dve.tensor_scalar(f1, f0, -1.0, None, ALU.mult))
            dve.tensor_tensor(f1, f1, f0, ALU.max).then_inc(S("lf_abs"), 1)
            L(dve.tensor_scalar(f2, f0, 0.0, -1.0, ALU.min, ALU.mult))
            dve.wait_ge(S("lf_ln"), 1)
            L(dve.tensor_tensor(f1, f1, f2, ALU.add))
            L(dve.memset(f0, 1.0))
            dve.tensor_tensor_scan(f2, f0, f1, 0.0, ALU.mult, ALU.add).then_inc(S("F_done"), 1)
            for g in range(8):
                dve.wait_ge(S("fox_sq"), g + 1)
                dve.tensor_reduce(qstat[:, g * 8:g * 8 + 8],
                                  junk[:, (g % 2) * 512:(g % 2) * 512 + 512].rearrange("p (h d) -> p h d", d=64), AX,
                                  ALU.add).then_inc(S("fox_ss"), 1)
            dve.wait_ge(S("fox_ss"), 8)
            dve.tensor_scalar(qstat[:, 64:128], qstat[:, 0:64], 1.0 / 64, EPS, ALU.mult, ALU.add).then_inc(S("fox_var"), 1)
            dve.wait_ge(S("fox_rstd"), 1)
            dve.wait_ge(S("fox_out"), since("fox_out") + 8)
            for g in range(8):
                v = qk[:, g, :].rearrange("p (h d) -> p h d", d=64)
                L(dve.tensor_tensor(v, v, qstat[:, 128 + g * 8:136 + g * 8].unsqueeze(2).to_broadcast([P, 8, 64]),
                                    ALU.mult))
            end_stage("dve", dve)
            for i in range(1, 8, 2):
                dve.wait_ge(S("fox_turned"), i + 1)
                fox_place(dve, i)
            end_stage("dve", dve)

        def fox_in_pool(pool):
            pool.wait_ge(S("fox_var"), 1)
            nc.gpsimd.tensor_tensor(qstat[:, 128:192], qstat[:, 64:128], halves64[:, :], ALU.pow).then_inc(
                S("fox_rstd"), 1)
            end_stage("pool", pool)
            end_stage("pool", pool)

        N2 = H2 * T

        def fox_pe(pe):
            pe.wait_ge(S("causal_in"), 16)
            for i in range(N2 + 2):
                if i < N2:
                    h, t = i // T, i % T
                    n = (t + 1) * P
                    if i >= 2:
                        pe.wait_ge(S("f2_masked"), since("f2_masked") + i - 1)
                    nc.tensor.matmul(ps[:, i % 2, 0:n], q2[:, h, t * P:t * P + P], k2[:, h // 2, 0:n],
                                     start=True, stop=False)
                    nc.tensor.matmul(ps[:, i % 2, n - P:n], ident[:, :], causal, start=False, stop=True).then_inc(
                        S("f2_scores"), 1)
                j = i - 1
                if 0 <= j < N2:
                    pe.wait_ge(S("f2_probs"), since("f2_probs") + j + 1)
                    if j >= 2:
                        pe.wait_ge(S("f2_pT"), since("f2_pT") + j - 1)
                    for c in range(j % T + 1):
                        last = nc.tensor.transpose(ps[:, 2 + j % 2, c * P:c * P + P], pr(j)[:, c * P:c * P + P],
                                                   ident[:, :])
                    last.then_inc(S("f2_turned"), 1)
                j = i - 2
                if j >= 0:
                    h = j // T
                    pe.wait_ge(S("f2_pT"), since("f2_pT") + j + 1)
                    if j >= 2:
                        pe.wait_ge(S("f2_out"), since("f2_out") + j - 1)
                    accumulate(ps[:, 4 + j % 2, 0:P],
                               [(pT2(j)[:, c * P:c * P + P], v2[:, c, (h // 2) * P:(h // 2) * P + P])
                                for c in range(j % T + 1)]).then_inc(S("f2_pv"), 1)
            end_stage("pe", pe)
            for f in range(4):
                for t in range(T):
                    last = nc.tensor.transpose(ps[:, f, t * P:t * P + P], o2[:, t, f * P:f * P + P], ident[:, :])
                last.then_inc(S("f2_oturned"), 1)
            end_stage("pe", pe)

        def fox_dve(dve):
            for i in range(N2 + 1):
                if i < N2:
                    h, t = i // T, i % T
                    n = (t + 1) * P
                    dve.wait_ge(S("f2_scores"), since("f2_scores") + i + 1)
                    if i >= 2:
                        dve.wait_ge(S("f2_probs"), since("f2_probs") + i - 1)
                    dve.tensor_tensor_reduce(out=sm(i)[:, 0:n], in0=ps[:, i % 2, 0:n], in1=Fb[:, h, 0:n], scale=-1.0,
                                             scalar=BIG, op0=ALU.add, op1=ALU.min,
                                             accum_out=nmax[:, i:i + 1]).then_inc(S("f2_masked"), 1)
                j = i - 1
                if j >= 0:
                    n = (j % T + 1) * P
                    dve.wait_ge(S("f2_turned"), since("f2_turned") + j + 1)
                    if j >= 2:
                        dve.wait_ge(S("f2_pv"), since("f2_pv") + j - 1)
                    dve.tensor_copy(pT2(j)[:, 0:n], ps[:, 2 + j % 2, 0:n]).then_inc(S("f2_pT"), 1)
                    dve.wait_ge(S("f2_probs"), since("f2_probs") + j + 1)
                    dve.reciprocal(rden[:, j:j + 1], den[:, j:j + 1]).then_inc(S("f2_rden"), 1)
            end_stage("dve", dve)
            for f in range(1, 4, 2):
                dve.wait_ge(S("f2_oturned"), f + 1)
                dve.tensor_copy(oT[:, f, :], ps[:, f, :])
            end_stage("dve", dve)

        def fox_act(act):
            for i in range(N2 + 2):
                if i < N2:
                    n = (i % T + 1) * P
                    act.wait_ge(S("f2_masked"), since("f2_masked") + i + 1)
                    if i >= 2:
                        act.wait_ge(S("f2_turned"), since("f2_turned") + i - 1)
                    nc.scalar.activation(pr(i)[:, 0:n], sm(i)[:, 0:n], ACT.Exp, bias=nmax[:, i:i + 1], scale=-1.0,
                                         accum_out=den[:, i:i + 1]).then_inc(S("f2_probs"), 1)
                j = i - 2
                if j >= 0:
                    h, t = j // T, j % T
                    act.wait_ge(S("f2_pv"), since("f2_pv") + j + 1)
                    act.wait_ge(S("f2_rden"), since("f2_rden") + j + 1)
                    nc.scalar.activation(o2[:, t, h * 64:h * 64 + 64], ps[:, 4 + j % 2, (h % 2) * 64:(h % 2) * 64 + 64],
                                         ACT.Identity, scale=rden[:, j:j + 1]).then_inc(S("f2_out"), 1)
            end_stage("act", act)
            for f in range(0, 4, 2):
                act.wait_ge(S("f2_oturned"), f + 1)
                nc.scalar.copy(oT[:, f, :], ps[:, f, :])
            end_stage("act", act)

        mixT = wk_(2048, KD, SEQ)
        sg = wk_(6144, 8, SEQ)

        def mix2_pe(pe):
            for f in range(KD):
                c, i = f // 4, f % 4
                for b, (nm, src, kt) in enumerate((("ga", hT, KD), ("gs", hT, KD), ("pa", oT, 4), ("ps", ysT, 4))):
                    if i == 0:
                        arrived(pe, f"{nm}{c}")
                    if f >= 2:
                        if b < 2:
                            pe.wait_ge(S("mx_sig"), 2 * (f - 2) + b + 1)
                        else:
                            pe.wait_ge(S("mx_prod"), 2 * (f - 2) + b - 1)
                    accumulate(ps[:, 4 * (f % 2) + b, :], [(weight(f"{nm}{c}")[:, k, i * P:i * P + P], src[:, k, :])
                                                           for k in range(kt)]).then_inc(S("mx_sum"), 1)
                if i == 3:
                    pe.wait_ge(S("mx_sum"), since("mx_sum") + 4 * (f + 1))
                    pe.sem_inc(S("w_used1"), 4)
            end_stage("pe", pe)
            residual_pe("r8", lambda k: mixT[:, k, :], ["w_out_20", "w_out_21"], 1)
            end_stage("pe", pe)

        def mix2_act(act):
            for f in range(KD):
                for b in range(2):
                    act.wait_ge(S("mx_sum"), since("mx_sum") + 4 * f + b + 1)
                    if f >= 2:
                        act.wait_ge(S("mx_prod"), 2 * (f - 2) + b + 1)
                    nc.scalar.activation(sg[:, 2 * (f % 2) + b, :], ps[:, 4 * (f % 2) + b, :], ACT.Sigmoid).then_inc(
                        S("mx_sig"), 1)
            end_stage("act", act)
            end_stage("act", act)

        def mix2_dve(dve):
            for f in range(KD):
                for b in range(2):
                    dve.wait_ge(S("mx_sig"), 2 * f + b + 1)
                    dve.wait_ge(S("mx_sum"), since("mx_sum") + 4 * f + b + 3)
                    if f >= 2:
                        dve.wait_ge(S("mx_mixed"), f - 1)
                    dve.tensor_tensor(sg[:, 4 + 2 * (f % 2) + b, :], sg[:, 2 * (f % 2) + b, :],
                                      ps[:, 4 * (f % 2) + 2 + b, :], ALU.mult).then_inc(S("mx_prod"), 1)
            end_stage("dve", dve)
            residual_dve("r8")
            end_stage("dve", dve)

        def mix2_pool(pool):
            for f in range(KD):
                pool.wait_ge(S("mx_prod"), 2 * (f + 1))
                nc.gpsimd.tensor_tensor(mixT[:, f, :], sg[:, 4 + 2 * (f % 2), :], sg[:, 5 + 2 * (f % 2), :],
                                        ALU.add).then_inc(S("mx_mixed"), 1)
            end_stage("pool", pool)
            end_stage("pool", pool)

        STAGES_TO_PART2 = STAGES_TO_MOE1 + 2
        STAGES_TO_MOE2 = STAGES_TO_MOE1 + 2 + 2 + 1 + 1 + 1 + 2 + 2 + 2 + 2

        @block.sync
        def _(sp):
            sp.dma_start(x[:, :, :], a["x"][0].rearrange("(t p) n -> p t n", p=P)).then_inc(S("x_in"), 16)
            for dst, src in ((cols[:, :], a["cols"]), (rows[:, :], a["rows"].to_broadcast([P, NROW])),
                             (ident[:, :], a["ident"]), (mask1[:, :], a["mask1"]),
                             (tri[:, :], a["tri"]), (tokid[:, :], a["tokid"]),
                             (posi[:, :], a["positions"].unsqueeze(0).to_broadcast([P, SEQ]))):
                sp.dma_start(dst, src).then_inc(S("par_in"), 16)
            load_part(sp, False)
            sp.wait_ge(S("stage_done"), 4 * STAGES_TO_MOE1)
            sp.dma_start(final_g, a["final_norm_g"].unsqueeze(0).to_broadcast([P, D])).then_inc(S("fg_in"), 16)
            moe_sp(sp, 6, a["w1"], a["w3"], a["w2"], FF1, 2)
            sp.wait_ge(S("stage_done"), 4 * STAGES_TO_PART2)
            load_part(sp, True)
            sp.wait_ge(S("stage_done"), 4 * STAGES_TO_MOE2)
            moe_sp(sp, 9, a["w_expert_gate_2"], a["w_expert_up_2"], a["w_expert_down_2"], FF2, 4)
            sp.wait_ge(S("final"), 1)
            sp.dma_start(out[0].rearrange("(t p) n -> p t n", p=P), x[:, :, :]).then_inc(S("out_stored"), 16)
            sp.wait_ge(S("out_stored"), 16)

        @block.tensor
        def _(pe):
            pe.wait_ge(S("par_in"), 16 * 7)
            stage1_pe(pe)
            attn1_pe(pe)
            mem_pe(pe)
            mix_pe(pe)
            residual_pe("r3", lambda k: hT[:, k, :], ["w_out0", "w_out1"], 0)
            end_stage("pe", pe)
            xattn_pe(pe)
            moe_route_pe(pe, 6)
            moe_pe(pe, 6, FF1, 2)
            for name in sorted(RECYCLED.values()):
                pe.sem_clear(S(name))
            end_stage("pe", pe)
            end_stage("pe", pe)
            norm_pe("n7", xn_tile, T)
            end_stage("pe", pe)
            s5_prep_pe(pe)
            s5_pe(pe)
            glu_pe(pe)
            fox_in_pe(pe)
            fox_pe(pe)
            mix2_pe(pe)
            moe_route_pe(pe, 9)
            moe_pe(pe, 9, FF2, 4)
            end_stage("pe", pe)

        @block.scalar
        def _(act):
            stage1_act(act)
            act.dma_start(memx, a["mem"][0].rearrange("(t p) n -> p t n", p=P)).then_inc(S("mem_in"), 16)
            attn1_act(act)
            mem_act(act)
            norm_act("nm", o1, AW, T, lambda k: hT[:, k, :], mix_gain)
            end_stage("act", act)
            end_stage("act", act)
            xattn_act(act)
            moe_route_act(act, 6, "moe_g")
            moe_act(act, 6, FF1, 2)
            end_stage("act", act)
            final_act(act)
            s5_prep_act(act)
            s5_act(act)
            glu_act(act)
            fox_in_act(act)
            fox_act(act)
            mix2_act(act)
            moe_route_act(act, 9, "ffn2_g")
            moe_act(act, 9, FF2, 4)
            end_stage("act", act)

        @block.vector
        def _(dve):
            stage1_dve(dve)
            attn1_dve(dve)
            mem_dve(dve)
            norm_dve("nm", o1, AW, T, o1, lambda k: hT[:, k, :], mix_gain)
            end_stage("dve", dve)
            residual_dve("r3")
            end_stage("dve", dve)
            xattn_dve(dve)
            moe_route_dve(dve, 6, "moe_g", "route_b1")
            moe_dve(dve, 6, FF1, "moe_g", 2)
            combine_dve(dve, 6)
            final_dve(dve)
            s5_prep_dve(dve)
            s5_dve(dve)
            glu_dve(dve)
            fox_in_dve(dve)
            fox_dve(dve)
            mix2_dve(dve)
            moe_route_dve(dve, 9, "ffn2_g", "route_b2")
            moe_dve(dve, 9, FF2, "ffn2_g", 4)
            combine_dve(dve, 9)
            dve.sem_inc(S("final"), 1)

        @block.gpsimd
        def _(pool):
            nc.gpsimd.memset(ones[:, :], 1.0)
            stage1_pool(pool)
            end_stage("pool", pool)
            mem_pool(pool)
            norm_pool("nm", T)
            end_stage("pool", pool)
            end_stage("pool", pool)
            xattn_pool(pool)
            moe_route_pool(pool, 6, a["w_group"][0], a["w_router"][0])
            moe_pool(pool, 6)
            combine_pool(pool, 6)
            norm_pool("nf", T)
            end_stage("pool", pool)
            norm_pool("n7", T)
            end_stage("pool", pool)
            s5_load_pool(pool)
            end_stage("pool", pool)
            s5_pool(pool)
            end_stage("pool", pool)
            fox_in_pool(pool)
            end_stage("pool", pool)
            end_stage("pool", pool)
            mix2_pool(pool)
            moe_route_pool(pool, 9, a["w_router_group_2"][0], a["w_router_expert_2"][0])
            moe_pool(pool, 9)
            combine_pool(pool, 9)


def columns(v, n):
    return np.asarray(v, np.float32).reshape(n, P).T


def host_arrays(i):
    f = lambda n: np.asarray(i[n])
    cols = np.zeros((P, NCOL), np.float32)

    def put(name, v):
        cols[:, COLS[name][0]:COLS[name][1]] = v

    put("mix_g", columns(f("mix_norm_g")[0], KD))
    put("xattn_g", columns(f("xattn_norm_g")[0], KD))
    put("mem_g", columns(f("mem_norm_g")[0], KD))
    put("moe_g", columns(f("moe_norm_g")[0], KD))
    put("conv_out_g", columns(f("conv_out_g")[0], 2))
    put("attn_out_g", columns(f("attn_out_g")[0], 6))
    put("dw_b", columns(f("conv_dw_b")[0], 2))
    put("dw_w", f("conv_dw_w")[0].reshape(TAPS, 2, P).transpose(2, 1, 0).reshape(P, 2 * TAPS))
    put("mix2_g", columns(f("norm_mix_g_2")[0], KD))
    put("ffn2_g", columns(f("norm_ffn_g_2")[0], KD))
    put("qn_g", np.tile(f("q_norm_g_2")[0], 2).reshape(P, 1))
    put("kn_g", np.tile(f("k_norm_g_2")[0], 2).reshape(P, 1))
    put("ssm_d", columns(f("ssm_D_2")[0], NU))
    put("a_re", columns(f("ssm_A_re_2")[0].reshape(-1), SS))
    put("a_im", columns(f("ssm_A_im_2")[0].reshape(-1), SS))
    put("log_dt", columns(np.repeat(f("ssm_log_dt_2")[0], 64), SS))
    cols[0:H2, COLS["forget_b"][0]] = f("b_forget_2")[0]
    half = np.arange(P) % 32
    put("inv_freq", (1.0 / (10000.0 ** (half.astype(np.float32) * np.float32(2.0 / 64)))).astype(np.float32).reshape(P, 1))
    put("group_of", (np.arange(P)[:, None] // 16 == np.arange(8)[None, :]).astype(np.float32))
    put("half", (np.arange(P)[:, None] // 64 == np.arange(2)[None, :]).astype(np.float32))
    rows = np.zeros((1, NROW), np.float32)

    def putr(name, v):
        rows[0, ROWS[name][0]:ROWS[name][1]] = v

    putr("ln_g", f("conv_ln_g")[0])
    putr("ln_b", f("conv_ln_b")[0])
    putr("route_b1", np.concatenate([f("b_group")[0], f("b_router")[0]]))
    putr("route_b2", np.concatenate([f("b_router_group_2")[0], f("b_router_expert_2")[0]]))
    putr("down_g", NG - np.arange(NG))
    putr("down_e", NE - np.arange(NE))
    putr("iota_slot", np.arange(SLOT))
    putr("iota_blk", SLOT * np.arange(NTAB + 1))
    putr("iota_chunk", 1 + np.arange(CH))
    diff = np.arange(P)[:, None] - np.arange(3 * P + SEQ)[None, :] + 3 * P
    c = (np.abs(diff) <= 64).astype(int) + ((np.abs(diff) <= 256) & (diff % 4 == 0)) + (diff % 16 == 0)
    mask1 = np.where(c > 0, np.log(np.maximum(c, 1)), -BIG).astype(np.float32)
    perm = np.zeros((P, P), np.float32)
    for o in range(P):
        if o % 64 < 32:
            perm[o + 32, o] = -1.0
        else:
            perm[o - 32, o] = 1.0
    tri = (np.arange(P)[:, None] < np.arange(P)[None, :]).astype(np.float32)
    tokid = (np.arange(P)[:, None] + P * np.arange(T)[None, :]).astype(np.float32)
    causal = np.where(np.arange(P)[None, :] <= np.arange(P)[:, None], 0.0, -BIG).astype(np.float32)
    out = dict(cols=cols, rows=rows, ident=np.eye(P, dtype=np.float32), mask1=mask1, perm=perm, tri=tri,
               tokid=tokid, causal=causal)
    for n in ("x", "mem", "positions", "w_in", "w_out", "w_xq", "w_xk", "w_xv", "w_xo", "w_group", "w_router",
              "w1", "w3", "w2", "w_in_2", "w_glu_2", "w_proj_attn_2", "w_proj_ssm_2", "w_out_2",
              "w_router_group_2", "w_router_expert_2", "w_expert_gate_2", "w_expert_up_2", "w_expert_down_2",
              "final_norm_g", "ssm_B_re_2", "ssm_B_im_2", "ssm_C_re_2", "ssm_C_im_2"):
        out[n] = np.ascontiguousarray(f(n))
    return out


def kernel(**inputs):
    import concourse.bacc as _bacc
    from concourse.bass_utils import run_bass_kernel_spmd as _run

    nc = _bacc.Bacc("TRN2", target_bir_lowering=False, num_devices=1)
    arrays = {f"in_{n}": v for n, v in host_arrays(inputs).items()}
    args = {n[3:]: nc.dram_tensor(n, v.shape, mybir.dt.from_np(v.dtype), kind="ExternalInput").ap()
            for n, v in arrays.items()}
    out = nc.dram_tensor("out", (1, SEQ, D), F32, kind="ExternalOutput").ap()
    build(nc, args, out)
    return _run(nc, [arrays], core_ids=[0]).results[0]["out"]
```
